# Optimizing a Trainium2 kernel written in Bass

```python
import math
import jax, jax.numpy as jnp
from jax import lax
import numpy as np

D_MODEL = 1024
BATCH = 1
SEQ = 512
DEPTH = 1
DEC_BATCH = 8
DEC_SEQ = 1
PAST_LEN = 4096
PAGE_SIZE = 128

MIX_WIDTH = D_MODEL
M_HEADS = 4
M_DV = MIX_WIDTH // 2 // M_HEADS
M_DK = M_DV // 2
M_CHUNK = 64
A_HEADS = 8
A_HD = MIX_WIDTH // 2 // A_HEADS
A_KV = 2
A_GROUP = A_HEADS // A_KV
WINDOW = 128
ATT_BLOCK = WINDOW
NUM_BUCKETS = 32
MAX_DISTANCE = 128
N_EXPERTS = 32
TOP_K = 4
D_FF = D_MODEL
SWIGLU_LIMIT = 7.0
SWIGLU_ALPHA = 1.702
MOE_BLOCK = 128
EPS = 1e-5
SPLITS = (M_HEADS * M_DK, M_HEADS * M_DK, M_HEADS * M_DV, M_HEADS * M_DV, M_HEADS, M_HEADS,
          A_HEADS * A_HD, A_KV * A_HD, A_KV * A_HD)
PROJ_DIM = sum(SPLITS)

kernel_name = "hymba_mlstm_swa_sink_moe_step"

F32 = jnp.float32

def rms_norm(x, g):
    xf = x.astype(F32)
    y = xf * lax.rsqrt(jnp.mean(xf * xf, axis=-1, keepdims=True) + EPS) * g.astype(F32)
    return y.astype(x.dtype)

def split_proj(xn, w_in, b_if):
    z = xn @ w_in
    offs, acc = [], 0
    for w in SPLITS[:-1]:
        acc += w
        offs.append(acc)
    mq, mk, mv, mo, mi, mf, aq, ak, av = jnp.split(z, offs, axis=-1)
    i_pre = (mi + b_if[:M_HEADS]).astype(F32)
    logf = jax.nn.log_sigmoid((mf + b_if[M_HEADS:]).astype(F32))
    return mq, mk, mv, mo, i_pre, logf, aq, ak, av

def mlstm_chunked(q, k, v, i_pre, logf, C0, n0, m0, chunk):
    B, T, H, _ = q.shape
    nc = T // chunk

    def to_chunks(a):
        a = a.astype(F32)
        return a.reshape((B, nc, chunk) + a.shape[2:]).swapaxes(0, 1)

    xs = tuple(to_chunks(a) for a in (q, k, v, i_pre, logf))
    causal = jnp.tril(jnp.ones((chunk, chunk), bool))

    def step(carry, inp):
        C, n, m = carry
        qc, kc, vc, ic, fc = inp
        b = jnp.cumsum(fc, axis=1)
        a = b + m[:, None, :]
        dmat = b[:, :, None, :] - b[:, None, :, :] + ic[:, None, :, :]
        dmat = jnp.where(causal[None, :, :, None], dmat, -jnp.inf)
        mt = jnp.maximum(a, jnp.max(dmat, axis=2))
        w_intra = jnp.exp(dmat - mt[:, :, None, :])
        w_inter = jnp.exp(a - mt)
        s = jnp.einsum('bthd,bshd->btsh', qc, kc) * w_intra
        num = (w_inter[..., None] * jnp.einsum('bthd,bhde->bthe', qc, C)
               + jnp.einsum('btsh,bshe->bthe', s, vc))
        qn = w_inter * jnp.einsum('bthd,bhd->bth', qc, n) + jnp.sum(s, axis=2)
        den = jnp.maximum(jnp.abs(qn), jnp.exp(-mt))
        h = num / den[..., None]
        bl = b[:, -1]
        m_new = mt[:, -1]
        g_prev = jnp.exp(bl + m - m_new)
        g_s = jnp.exp(bl[:, None] - b + ic - m_new[:, None])
        C_new = g_prev[..., None, None] * C + jnp.einsum('bsh,bshd,bshe->bhde', g_s, kc, vc)
        n_new = g_prev[..., None] * n + jnp.einsum('bsh,bshd->bhd', g_s, kc)
        return (C_new, n_new, m_new), h

    (C, n, m), hs = lax.scan(step, (C0.astype(F32), n0.astype(F32), m0.astype(F32)), xs)
    h = hs.swapaxes(0, 1).reshape(B, T, H, v.shape[-1])
    return h, C, n, m

def mlstm_mix(mq, mk, mv, mo, i_pre, logf, C0, n0, m0, m_gain, chunk):
    B, T, _ = mq.shape
    q = mq.reshape(B, T, M_HEADS, M_DK)
    k = mk.reshape(B, T, M_HEADS, M_DK) * (M_DK ** -0.5)
    v = mv.reshape(B, T, M_HEADS, M_DV)
    h, C, n, m = mlstm_chunked(q, k, v, i_pre, logf, C0, n0, m0, chunk)
    hn = h * lax.rsqrt(jnp.mean(h * h, axis=-1, keepdims=True) + EPS) * m_gain.astype(F32).reshape(M_HEADS, M_DV)
    out = hn * jax.nn.sigmoid(mo.astype(F32).reshape(B, T, M_HEADS, M_DV))
    return out.reshape(B, T, M_HEADS * M_DV).astype(mq.dtype), C, n, m

def t5_bucket(dist):
    n = jnp.maximum(dist, 0)
    max_exact = NUM_BUCKETS // 2
    large = max_exact + (jnp.log(jnp.maximum(n, 1).astype(F32) / max_exact)
                         / math.log(MAX_DISTANCE / max_exact) * (NUM_BUCKETS - max_exact)).astype(jnp.int32)
    large = jnp.minimum(large, NUM_BUCKETS - 1)
    return jnp.where(n < max_exact, n, large)

def sink_window_attention(q, k, v, dist, valid, rel_bias, sinks):
    N, Lq, Lk = dist.shape
    logits = jnp.einsum('bnqhgd,bnshd->bnhgqs', q, k).astype(F32) * (A_HD ** -0.5)
    bias = rel_bias.astype(F32)[t5_bucket(dist)]
    bias = bias.reshape(N, Lq, Lk, A_KV, A_GROUP).transpose(0, 3, 4, 1, 2)
    logits = jnp.where(valid[:, None, None], logits + bias[None], -jnp.inf)
    sink = jnp.broadcast_to(sinks.astype(F32).reshape(A_KV, A_GROUP, 1, 1), logits.shape[:-1] + (1,))
    probs = jax.nn.softmax(jnp.concatenate([logits, sink], axis=-1), axis=-1)[..., :-1]
    return jnp.einsum('bnhgqs,bnshd->bnqhgd', probs.astype(v.dtype), v)

def attn_prompt(aq, ak, av, rel_bias, sinks):
    B, T, _ = aq.shape
    nb = T // ATT_BLOCK
    q = aq.reshape(B, nb, ATT_BLOCK, A_KV, A_GROUP, A_HD)
    k = ak.reshape(B, nb, ATT_BLOCK, A_KV, A_HD)
    v = av.reshape(B, nb, ATT_BLOCK, A_KV, A_HD)
    padw = ((0, 0), (1, 0), (0, 0), (0, 0), (0, 0))
    k2 = jnp.concatenate([jnp.pad(k, padw)[:, :-1], k], axis=2)
    v2 = jnp.concatenate([jnp.pad(v, padw)[:, :-1], v], axis=2)
    blk = jnp.arange(nb, dtype=jnp.int32)[:, None]
    qpos = blk * ATT_BLOCK + jnp.arange(ATT_BLOCK, dtype=jnp.int32)[None]
    kpos = (blk - 1) * ATT_BLOCK + jnp.arange(2 * ATT_BLOCK, dtype=jnp.int32)[None]
    dist = qpos[:, :, None] - kpos[:, None, :]
    valid = (dist >= 0) & (dist <= WINDOW) & (kpos[:, None, :] >= 0)
    o = sink_window_attention(q, k2, v2, dist, valid, rel_bias, sinks)
    new_k = ak.reshape(B, T, A_KV, A_HD)[:, -WINDOW:]
    new_v = av.reshape(B, T, A_KV, A_HD)[:, -WINDOW:]
    return o.reshape(B, T, A_HEADS * A_HD), new_k, new_v

def attn_sample(aq, ak, av, cache_k, cache_v, rel_bias, sinks):
    B, T, _ = aq.shape
    W = cache_k.shape[1]
    q = aq.reshape(B, 1, T, A_KV, A_GROUP, A_HD)
    k_all = jnp.concatenate([cache_k.astype(ak.dtype), ak.reshape(B, T, A_KV, A_HD)], axis=1)
    v_all = jnp.concatenate([cache_v.astype(av.dtype), av.reshape(B, T, A_KV, A_HD)], axis=1)
    qpos = PAST_LEN + jnp.arange(T, dtype=jnp.int32)
    kpos = PAST_LEN - W + jnp.arange(W + T, dtype=jnp.int32)
    dist = (qpos[:, None] - kpos[None, :])[None]
    valid = (dist >= 0) & (dist <= WINDOW) & (kpos[None, None, :] >= 0)
    o = sink_window_attention(q, k_all[:, None], v_all[:, None], dist, valid, rel_bias, sinks)
    return o.reshape(B, T, A_HEADS * A_HD), k_all[:, -W:], v_all[:, -W:]

def moe(xn, w_router, b_router, w_gate, b_gate, w_up, b_up, w_down, b_down):
    B, T, D = xn.shape
    x2 = xn.reshape(-1, D)
    N = x2.shape[0]
    nk = N * TOP_K
    logits = (x2 @ w_router + b_router).astype(F32)
    top_val, top_idx = lax.top_k(logits, TOP_K)
    gates = jax.nn.softmax(top_val, axis=-1)
    flat_e = top_idx.reshape(-1)
    flat_g = gates.reshape(-1)
    order = jnp.argsort(flat_e)
    sorted_e = flat_e[order]
    counts = jnp.bincount(flat_e, length=N_EXPERTS)
    padded = (counts + MOE_BLOCK - 1) // MOE_BLOCK * MOE_BLOCK
    pad_end = jnp.cumsum(padded)
    pad_start = pad_end - padded
    start = jnp.cumsum(counts) - counts
    dest = pad_start[sorted_e] + jnp.arange(nk) - start[sorted_e]
    n_blocks = (nk + N_EXPERTS * (MOE_BLOCK - 1) + MOE_BLOCK - 1) // MOE_BLOCK
    rows = n_blocks * MOE_BLOCK
    row_tok = jnp.zeros((rows,), jnp.int32).at[dest].set((order // TOP_K).astype(jnp.int32))
    row_w = jnp.zeros((rows,), F32).at[dest].set(flat_g[order])
    block_e = jnp.minimum(jnp.searchsorted(pad_end, jnp.arange(n_blocks) * MOE_BLOCK, side='right'),
                          N_EXPERTS - 1)
    xs = x2[row_tok].reshape(n_blocks, MOE_BLOCK, D)

    def expert_block(args):
        xb, e = args
        g = xb @ w_gate[e] + b_gate[e]
        u = xb @ w_up[e] + b_up[e]
        g = jnp.minimum(g, SWIGLU_LIMIT)
        u = jnp.clip(u, -SWIGLU_LIMIT, SWIGLU_LIMIT)
        h = (u + 1) * (g * jax.nn.sigmoid(SWIGLU_ALPHA * g))
        return h @ w_down[e] + b_down[e]

    out = lax.map(expert_block, (xs, block_e))
    y = jax.ops.segment_sum(out.reshape(rows, D).astype(F32) * row_w[:, None], row_tok, num_segments=N)
    return y.astype(xn.dtype).reshape(B, T, D)

def setup_inputs(seed: int = 0) -> dict:
    key = jax.random.key(seed)
    ks = jax.random.split(key, 32)
    cache_win = min(WINDOW, PAST_LEN)
    nrm = lambda k, s, sc: jax.random.normal(k, s, F32) * sc
    f_bias = jnp.linspace(3.0, 6.0, M_HEADS, dtype=F32)[None] + nrm(ks[10], (DEPTH, M_HEADS), 0.1)
    i_bias = nrm(ks[11], (DEPTH, M_HEADS), 0.1)
    return {
        "x_prompt": nrm(ks[0], (BATCH, SEQ, D_MODEL), 1.0),
        "x_sample": nrm(ks[1], (DEC_BATCH, DEC_SEQ, D_MODEL), 1.0),
        "state_C": nrm(ks[2], (DEPTH, DEC_BATCH, M_HEADS, M_DK, M_DV), 0.1),
        "state_n": nrm(ks[3], (DEPTH, DEC_BATCH, M_HEADS, M_DK), 0.1),
        "state_m": nrm(ks[4], (DEPTH, DEC_BATCH, M_HEADS), 1.0),
        "cache_k": nrm(ks[5], (DEPTH, DEC_BATCH, cache_win, A_KV, A_HD), 1.0),
        "cache_v": nrm(ks[6], (DEPTH, DEC_BATCH, cache_win, A_KV, A_HD), 1.0),
        "rel_bias": nrm(ks[7], (NUM_BUCKETS, A_HEADS), 0.1),
        "norm1": 1.0 + nrm(ks[8], (DEPTH, D_MODEL), 0.02),
        "w_in": nrm(ks[9], (DEPTH, D_MODEL, PROJ_DIM), D_MODEL ** -0.5),
        "b_if": jnp.concatenate([i_bias, f_bias], axis=-1),
        "m_gain": 1.0 + nrm(ks[12], (DEPTH, M_HEADS * M_DV), 0.02),
        "sinks": nrm(ks[13], (DEPTH, A_HEADS), 0.5),
        "w_out": nrm(ks[14], (DEPTH, MIX_WIDTH, D_MODEL), MIX_WIDTH ** -0.5),
        "norm2": 1.0 + nrm(ks[15], (DEPTH, D_MODEL), 0.02),
        "w_router": nrm(ks[16], (DEPTH, D_MODEL, N_EXPERTS), D_MODEL ** -0.5),
        "b_router": nrm(ks[17], (DEPTH, N_EXPERTS), 0.01),
        "w_gate": nrm(ks[18], (DEPTH, N_EXPERTS, D_MODEL, D_FF), D_MODEL ** -0.5),
        "b_gate": nrm(ks[19], (DEPTH, N_EXPERTS, D_FF), 0.01),
        "w_up": nrm(ks[20], (DEPTH, N_EXPERTS, D_MODEL, D_FF), D_MODEL ** -0.5),
        "b_up": nrm(ks[21], (DEPTH, N_EXPERTS, D_FF), 0.01),
        "w_down": nrm(ks[22], (DEPTH, N_EXPERTS, D_FF, D_MODEL), D_FF ** -0.5),
        "b_down": nrm(ks[23], (DEPTH, N_EXPERTS, D_MODEL), 0.01),
        "final_norm": 1.0 + nrm(ks[24], (D_MODEL,), 0.02),
    }

def reference(x_prompt, x_sample, state_C, state_n, state_m, cache_k, cache_v, rel_bias,
              norm1, w_in, b_if, m_gain, sinks, w_out, norm2, w_router, b_router,
              w_gate, b_gate, w_up, b_up, w_down, b_down, final_norm):
    yp, ys = x_prompt, x_sample
    Bp = x_prompt.shape[0]
    pC, pn, pm, pk, pv = [], [], [], [], []
    sC, sn, sm, sk, sv = [], [], [], [], []
    for l in range(DEPTH):
        mq, mk, mv, mo, i_pre, logf, aq, ak, av = split_proj(rms_norm(yp, norm1[l]), w_in[l], b_if[l])
        zC = jnp.zeros((Bp, M_HEADS, M_DK, M_DV), F32)
        zn = jnp.zeros((Bp, M_HEADS, M_DK), F32)
        zm = jnp.zeros((Bp, M_HEADS), F32)
        m_out, C1, n1, m1 = mlstm_mix(mq, mk, mv, mo, i_pre, logf, zC, zn, zm, m_gain[l], M_CHUNK)
        a_out, k1, v1 = attn_prompt(aq, ak, av, rel_bias, sinks[l])
        yp = yp + jnp.concatenate([m_out, a_out], axis=-1) @ w_out[l]
        yp = yp + moe(rms_norm(yp, norm2[l]), w_router[l], b_router[l], w_gate[l], b_gate[l],
                      w_up[l], b_up[l], w_down[l], b_down[l])
        pC.append(C1); pn.append(n1); pm.append(m1); pk.append(k1); pv.append(v1)
        mq, mk, mv, mo, i_pre, logf, aq, ak, av = split_proj(rms_norm(ys, norm1[l]), w_in[l], b_if[l])
        m_out, C2, n2, m2 = mlstm_mix(mq, mk, mv, mo, i_pre, logf, state_C[l], state_n[l], state_m[l],
                                      m_gain[l], ys.shape[1])
        a_out, k2, v2 = attn_sample(aq, ak, av, cache_k[l], cache_v[l], rel_bias, sinks[l])
        ys = ys + jnp.concatenate([m_out, a_out], axis=-1) @ w_out[l]
        ys = ys + moe(rms_norm(ys, norm2[l]), w_router[l], b_router[l], w_gate[l], b_gate[l],
                      w_up[l], b_up[l], w_down[l], b_down[l])
        sC.append(C2); sn.append(n2); sm.append(m2); sk.append(k2); sv.append(v2)
    yp = rms_norm(yp, final_norm)
    ys = rms_norm(ys, final_norm)
    p_C, p_n, p_m = jnp.stack(pC), jnp.stack(pn), jnp.stack(pm)
    p_k, p_v = jnp.stack(pk), jnp.stack(pv)
    s_C, s_n, s_m = jnp.stack(sC), jnp.stack(sn), jnp.stack(sm)
    s_k, s_v = jnp.stack(sk), jnp.stack(sv)
    return (yp, ys, p_C, p_n, p_m, p_k, p_v, s_C, s_n, s_m, s_k, s_v)


_drawn_inputs = setup_inputs


def setup_inputs(seed=0):
    import zlib

    import numpy as np

    out = dict(_drawn_inputs(seed))
    spreads = {}
    factors = {'sinks': 8.0, 'b_gate': 8.0, 'b_up': 8.0, 'b_down': 8.0, 'final_norm': 2.844}
    for name, (base, spread) in spreads.items():
        noise = np.random.default_rng([zlib.crc32(name.encode()), seed]).standard_normal(out[name].shape)
        drawn = base * np.exp(spread * noise) if base else spread * noise
        out[name] = __import__('jax').numpy.asarray(drawn.astype(out[name].dtype))
    for name, factor in factors.items():
        out[name] = (out[name] * factor).astype(out[name].dtype)
    return out
```

```python
from contextlib import ExitStack

import concourse.bass as bass
from concourse import mybir

F32 = mybir.dt.float32
F32R = mybir.dt.float32r
I32 = mybir.dt.int32
U32 = mybir.dt.uint32
ALU = mybir.AluOpType
ACT = mybir.ActivationFunctionType
AX_X = mybir.AxisListType.X

P = 128
D = 1024
KC = D // P
T = 512
NB = 8
TT = T + NB
NT = T // P
NTILE = NT + 1
HALF = TT // 2
MH, DK, DV = 4, 64, 128
AH, KV, HD = 8, 2, 64
GRP = AH // KV
WIN = 128
NE, TOPK = 32, 4
CAP = 96
PASSES = -(-TT // CAP)
RING = 8
HIS = 4
N_PIECE = 12
AHEAD = 3
PIECE = 2048
N_IN = 9
N_OUT = 4
N_FIRST = N_IN + N_OUT
EPS = 1e-5
LIMIT, ALPHA = 7.0, 1.702
NEG = -1e30
RLEN = 383
NBUCKET, MAXDIST = 32, 128
BIG = 1.0e6
ROWS = TT * TOPK
EARLY = 2

FINAL = [NT] + list(range(NT))

ZQ, ZK, ZV, ZO, ZAQ, ZAK, ZAV, NZ = 0, 2, 4, 8, 12, 16, 17, 18


def rows(i):
    return P if i < NT else NB


def count_passes(most):
    return (most + (CAP - 1)) // CAP


def alone(eng, sem, value):
    value = eng.to_reg(value)
    eng.wait_ge(sem, 1)
    eng.wait_ge(sem, value)


def bucket_starts():
    half = NBUCKET // 2
    ratio = (MAXDIST / half) ** (1.0 / (NBUCKET - half))
    starts = list(range(half))
    for b in range(NBUCKET - half):
        edge = half * ratio ** b
        starts.append(half if b == 0 else int(edge) + 1)
    return starts + [MAXDIST + 1]


def hybrid_step(nc, a, o):
    with ExitStack() as ctx:
        end_of = {}

        def sb(name, shape, dt=F32):
            t = ctx.enter_context(nc.sbuf_tensor(name, shape, dt))
            end_of[name] = nc.sbuf_base
            return t

        def split_view(region, words, first, shape):
            return nc.alloc_sbuf_tensor_at(f"{region}_r{first}", shape, F32R, offset=end_of[region] - 4 * (words - first))

        def sem(name):
            return ctx.enter_context(nc.semaphore(name))

        ring = sb("ring", [P, RING + HIS, PIECE])
        reg_a = sb("reg_a", [P, KC * TT])
        reg_z = sb("reg_z", [P, NZ * TT])
        reg_x = sb("reg_x", [P, 2048])
        reg_t = sb("reg_t", [P, 4120])
        reg_b = sb("reg_b", [P, 2048])
        reg_w = sb("reg_w", [P, 2048])
        reg_p = sb("reg_p", [P, 1536])
        reg_c = sb("reg_c", [P, 2304])

        xnT = reg_a[:, :].rearrange("p (c t) -> p c t", c=KC)
        xnT_hi = split_view("reg_a", KC * TT, 0, [P, KC * TT])[:, :].rearrange("p (c t) -> p c t", c=KC)
        mixT = xnT
        xg = reg_a[:, 0:2048].rearrange("p (b n) -> p b n", b=2)
        yrow = reg_a[:, 2048:4096].rearrange("p (b n) -> p b n", b=2)
        zT = reg_z[:, :].rearrange("p (c t) -> p c t", c=NZ)
        y1 = reg_z[:, 0:NTILE * D].rearrange("p (i n) -> p i n", i=NTILE)
        z0 = NTILE * D
        eX, eH = (split_view("reg_z", NZ * TT, z0 + n, [P, 2 * KC * CAP])[:, :].rearrange(
            "p (b c n) -> p b c n", b=2, c=KC) for n in (0, 2 * KC * CAP))
        n2_bc = reg_z[:, z0:z0 + D]
        xbuf = reg_x[:, :].rearrange("p (b n) -> p b n", b=2)
        hrow = reg_x[:, 0:D]
        c_state = reg_z[:, ZV * TT:ZV * TT + 2048]
        c_prod = reg_x[:, :]
        v_tok = reg_t[:, 0:2064].rearrange("p (i h n) -> p i h n", i=NT, h=MH)
        k_tok = reg_t[:, 2064:3088].rearrange("p (i n) -> p i n", i=NT)
        av_tok = reg_t[:, 3088:3600].rearrange("p (i n) -> p i n", i=NT)
        ak_swap = reg_t[:, 3600:3600 + 512]
        route_v = reg_t[:, 0:NTILE * 33 * 3].rearrange("p (i e c) -> p i e c", i=NTILE, e=33)
        rank = reg_t[:, 500:500 + NTILE * 33].rearrange("p (i e) -> p i e", i=NTILE)
        chosen = reg_t[:, 680:680 + NTILE * NE].rearrange("p (i e) -> p i e", i=NTILE)
        onehot = reg_t[:, 840:840 + 2 * NTILE * CAP].rearrange("p (b i n) -> p b i n", b=2, i=NTILE)
        iota_cap = reg_t[:, 2120:2120 + CAP]
        iota_e = reg_t[:, 2250:2250 + NE]
        tok_k = reg_t[:, 2290:2290 + NTILE * TOPK].rearrange("p (i k) -> p i k", i=NTILE)
        rt_oh = reg_t[:, 2320:2320 + P].rearrange("p (e k) -> p e k", e=NE)
        rt_tmp = reg_t[:, 2450:2450 + P].rearrange("p (e k) -> p e k", e=NE)
        sums = reg_t[:, 2320:2320 + NTILE * NE].rearrange("p (i e) -> p i e", i=NTILE)
        lg = reg_t[:, 2580:2612]
        top8 = reg_t[:, 2620:2628]
        idxf = reg_t[:, 2628:2636]
        gexp = reg_t[:, 2636:2640]
        gate4 = reg_t[:, 2640:2644]
        rs1 = reg_t[:, 2644:2652]
        br_bc = reg_t[:, 2656:2688]
        count_f = reg_t[:, 2690:2691]
        id64 = reg_t[0:64, 3990:3990 + NE + 1]
        e_bias = [reg_t[0:64, 2960:3984], reg_c[0:64, 0:D], reg_w[0:64, 1024:2048]]
        e_bias_r = [split_view("reg_t", 4120, 2960, [64, D]), split_view("reg_c", 2304, 0, [64, D]),
                    split_view("reg_w", 2048, 1024, [64, D])]
        tmp_r = [split_view("reg_c", 2304, D, [64, D]), split_view("reg_z", NZ * TT, z0 + 3 * D, [64, D])]
        e_bias_tmp_r = [tmp_r[0][32:64, :], tmp_r[1][32:64, :], tmp_r[0][32:64, :]]
        pick = split_view("reg_p", 1536, 1280, [64, 2 * CAP])[:, :].rearrange("p (b n) -> p b n", b=2)
        zs = reg_b[0:NB, 0:1800]
        bias = reg_b[:, :].rearrange("p (h k) -> p h k", h=AH)
        xhat = reg_b[:, :].rearrange("p (b n) -> p b n", b=2)
        wexp = reg_w[:, 0:1024].rearrange("p (b n) -> p b n", b=2)
        neg_m = reg_w[:, 1024:1536]
        h_rows = [reg_b[:, 512 * n:512 * n + 512] for n in range(4)]
        h_ss = reg_w[:, 1770:1786]
        exp_m = reg_w[:, 1786:1802].rearrange("p (i h) -> p i h", i=NT)
        h_sq = reg_x[:, 1024:1536].rearrange("p (i n) -> p i n", i=NT)
        kg = reg_p[:, 1152:1408].rearrange("p (i k) -> p i k", i=NT)
        g_rows = [reg_w[0:8, 512 * n:512 * n + 512] for n in range(4)]
        mix_s = reg_w[0:NB, 0:D]
        x2T = reg_w[:, 0:1024].rearrange("p (c t) -> p c t", c=KC)
        prob = reg_p[:, 0:512].rearrange("p (b k) -> p b k", b=2)
        probT = reg_p[:, 512:1024].rearrange("p (b k) -> p b k", b=2)
        o_tok = reg_p[:, 1024:1536]
        bias_rows = reg_p[0:AH, 0:RLEN]
        relT = reg_p[0:AH, 400:432]
        fn_bc = reg_p[:, 0:D]
        w_rt = reg_p[:, D:D + KC * NE].rearrange("p (c e) -> p c e", c=KC)
        cache_ks = reg_c[:, 0:1024].rearrange("p (b n) -> p b n", b=NB)
        cache_vs = reg_c[:, 1024:2048].rearrange("p (b n) -> p b n", b=NB)
        kT_s = reg_c[:, 2048:2304].rearrange("p (b n) -> p b n", b=2)
        eG, eS = reg_b[:, 0:D], reg_b[:, D:2 * D]
        y_all = ring[:, 0:10, :].rearrange("p (i s) n -> p i (s n)", s=2)
        xnT_lo = [split_view(region, words, first, [P, TT]) for region, words, first in
                  [("reg_c", 2304, TT * c) for c in range(4)] + [("reg_b", 2048, TT * c) for c in range(3)]
                  + [("reg_t", 4120, 3600)]]
        gates = sb("gates", [8, TT])

        ident = sb("ident", [P, P])
        ones = reg_t[:, 2700:2828]
        tri = reg_t[:, 2830:2958]
        cols = sb("cols", [P, 20])
        small = sb("small", [P, 96])
        ssq = small[:, 0:8]
        sink_bc = small[:, 16:24]
        amax, nmax, asum, asnk = small[:, 24:32], small[:, 32:40], small[:, 40:48], small[:, 48:56]
        u_tok = small[:, 56:72].rearrange("p (i h) -> p i h", i=NT)
        nm_tok = small[:, 72:88].rearrange("p (i h) -> p i h", i=NT)
        b_if = small[0:8, 88:89]
        eps_col = small[:, 89:90]
        gsc = sb("gsc", [P, 24])
        d_in = reg_t[:, 400:464]
        q16, k16, n16, kw16 = d_in[:, 0:16], d_in[:, 16:32], d_in[:, 32:48], d_in[:, 48:64]
        part = reg_t[:, 0:132]
        part2 = part[:, 0:130]
        vrep = reg_t[:, 132:264]
        dl = reg_t[0:64, 264:400]
        ds = sb("ds", [64, 24])
        wif_v = reg_p[:, 960:1024].rearrange("p (c n) -> p c n", c=KC)
        wif_r = split_view("reg_p", 1536, 1152, [P, 128])[:, :].rearrange("p (b c n) -> p b c n", b=2, c=KC)
        ring_r = split_view("ring", (RING + HIS) * PIECE, 0, [P, (RING + HIS) * PIECE])[:, :].rearrange(
            "p (s n) -> p s n", s=RING + HIS)
        idx8 = sb("idx8", [P, 8], U32)
        slot_tok = sb("slot_tok", [P, 2], U32)
        slot_dst = sb("slot_dst", [P, 2], U32)
        slot_gate = sb("slot_gate", [P, 2])
        slot_tmp = sb("slot_tmp", [P, 2])
        count_i = sb("count_i", [1, 1], I32)
        r32 = reg_w[0:32, 0:136]
        d32 = reg_w[0:32, 136:160]
        h_state = [reg_x[0:DK, h * (DV + 1):(h + 1) * (DV + 1)] for h in range(MH)]
        ak_last = reg_p[:, 1024:1152]
        junk = reg_c[:, D:2 * D]
        h32 = reg_w[0:32, 160:288]
        s32 = reg_w[0:32, 288:416]
        q64 = reg_w[0:64, 416:480]
        q2 = reg_w[0:64, 480:608]
        kv16 = reg_w[0:16, 608:736]
        kvown = reg_w[0:64, 736:864]
        qbd = reg_w[:, 864:928]
        sT = reg_w[:, 928:992]
        pT = reg_w[:, 992:1056]
        oT = reg_w[:, 1056:1120]
        o64 = reg_w[0:64, 1120:1248]
        a64 = reg_w[0:64, 1248:1312]
        m32 = reg_w[0:32, 1312:1313]
        gpre = reg_w[0:32, 1314:1316]
        brow9 = reg_w[0:AH, 1320:1452]
        g4 = reg_w[:, 1460:1492]
        r4 = reg_w[0:32, 1500:1628]
        r8 = reg_w[0:8, 1640:1704]
        kvm = reg_w[0:64, 1710:1712]
        kvi = sb("kvi", [64, 2], I32)
        negsel = reg_p[0:4, 432:944]

        ps = [ctx.enter_context(nc.psum_tensor(f"ps{n}", [P, 512], F32)) for n in range(8)]

        def dram(name, shape):
            return nc.dram_tensor(name, shape, F32).ap()

        sc_bias = dram("sc_bias", (AH, P * RLEN))
        sc_q, sc_k, sc_v = dram("sc_q", (NB, 256)), dram("sc_k", (NB, 256)), dram("sc_v", (NB, 512))
        sc_aq, sc_kv = dram("sc_aq", (NB, 512)), dram("sc_kv", (2, NB, 128))
        sc_gate = dram("sc_gate", (2, NB, MH))
        sc_mix = dram("sc_mix", (2, NB, 512))
        xhat_rows = dram("xhat_rows", (TT, D))
        moe_rows = dram("moe_rows", (ROWS, D))

        piece_in = [sem(f"piece_in_{s}") for s in range(RING)]
        pieces_used = sem("pieces_used")
        x_in = [sem("x_in_0"), sem("x_in_1")]
        consts_in, relT_in, cache_in = sem("consts_in"), sem("relT_in"), sem("cache_in")
        ident_made, masks_made, rows_made, iotas_made = sem("ident_made"), sem("masks_made"), sem("rows_made"), sem("iotas_made")
        eps_made, rms_ready = sem("eps_made"), sem("rms_ready")
        xn_ready, xT_psum, xT_ready = sem("xn_ready"), sem("xT_psum"), sem("xT_ready")
        w_hi, w_lo = sem("w_hi"), sem("w_lo")
        proj_psum, proj_ready = sem("proj_psum"), sem("proj_ready")
        tok_psum, tok_ready = sem("tok_psum"), sem("tok_ready")
        aksw_in = sem("aksw_in")
        gate_pe, gate_dve, lnf_ready = sem("gate_pe"), sem("gate_dve"), sem("lnf_ready")
        cols_psum, f_psum, gtok_psum = ((gate_pe, n + 1) for n in range(3))
        absf_ready, grows_ready, gtok_ready = ((gate_dve, n + 1) for n in range(3))
        negm_psum, gs_ready, kg_ready, expm_ready = sem("negm_psum"), sem("gs_ready"), sem("kg_ready"), sem("expm_ready")
        score_psum, wpre_ready, wexp_ready = sem("score_psum"), sem("wpre_ready"), sem("wexp_ready")
        wmask_ready, wgt_ready, num_kb, num_psum = sem("wmask_ready"), sem("wgt_ready"), sem("num_kb"), sem("num_psum")
        state_psum, state_ready, state_out = sem("state_psum"), sem("state_ready"), sem("state_out")
        num_used, hss_ready, hrms_ready, hn_ready = sem("num_used"), sem("hss_ready"), sem("hrms_ready"), sem("hn_ready")
        hT_psum, mixm_ready = sem("hT_psum"), sem("mixm_ready")
        out_done, pk_out = sem("out_done"), sem("pk_out")
        bias_out, bias_in = sem("bias_out"), sem("bias_in")
        s_psum, logit_ready, prob_ready = sem("s_psum"), sem("logit_ready"), sem("prob_ready")
        pT_psum, pT_ready, pv_psum = sem("pT_psum"), sem("pT_ready"), sem("pv_psum")
        sinkin_ready, sinkexp_ready = sem("sinkin_ready"), sem("sinkexp_ready")
        otok_ready, oT_psum, mixa_ready = sem("otok_ready"), sem("oT_psum"), sem("mixa_ready")
        sample_dve, sample_act, sample_pe = sem("sample_dve"), sem("sample_act"), sem("sample_pe")
        (dabs_ready, q2_ready, dpart_ready, dm_ready, dstate_ready, dss_ready, dh_ready, qbd_ready, dlogit_ready,
         datt_ready) = ((sample_dve, n + 1) for n in range(10))
        dln_ready, dw_ready, vrep_ready, sT_ready, dprob_ready, dpT_ready, doT_ready = (
            (sample_act, n + 1) for n in range(7))
        rep_psum, dsum_psum, own_psum, srow_psum, dpT_psum, do_psum, orow_psum = (
            (sample_pe, n + 1) for n in range(7))
        drms_ready = sem("drms_ready")
        zs_psum, zs_ready, zs_out, dec_in = sem("zs_psum"), sem("zs_ready"), sem("zs_out"), sem("dec_in")
        dstate_out = sem("dstate_out")
        kc_psum, kc_ready, ks_psum = sem("kc_psum"), sem("kc_ready"), sem("ks_psum")
        mixs_out, mixs_in, mixs_psum, mixs_ready = sem("mixs_out"), sem("mixs_in"), sem("mixs_psum"), sem("mixs_ready")
        xr_in = [sem("xr_in_0"), sem("xr_in_1")]
        early_psum, early_ready, early_x = sem("early_psum"), sem("early_ready"), sem("early_x")
        y_psum, y_ready, rms2_ready = sem("y_psum"), sem("y_ready"), sem("rms2_ready")
        xhat_ready, xhat_out = sem("xhat_ready"), [sem("xhat_out_0"), sem("xhat_out_1")]
        x2_psum, x2_ready = sem("x2_psum"), sem("x2_ready")
        lg_psum, top_ready, gexp_ready = sem("lg_psum"), sem("top_ready"), sem("gexp_ready")
        sel_ready, rank_psum, count_ready = sem("sel_ready"), sem("rank_psum"), sem("count_ready")
        late_in, bias_rows_in = sem("late_in"), sem("bias_rows_in")
        bias_hi, bias_lo = sem("bias_hi"), sem("bias_lo")
        onehot_ready, list_psum, slots_ready = sem("onehot_ready"), sem("list_psum"), sem("slots_ready")
        rows_in = [sem("rows_in_0"), sem("rows_in_1")]
        ex_psum, xhi_ready, ex_ready = sem("ex_psum"), sem("xhi_ready"), sem("ex_ready")
        hi_ready = sem("hi_ready")
        lo_ready = sem("lo_ready")
        pick_ready, g_ready, sg_ready, yrow_ready = sem("pick_ready"), sem("g_ready"), sem("sg_ready"), sem("yrow_ready")
        h_ready, hT_psum2, hhi_ready, hlo_ready = sem("h_ready"), sem("hT_psum2"), sem("hhi_ready"), sem("hlo_ready")
        rows_out = [sem("rows_out_0"), sem("rows_out_1")]
        last_in = [sem(f"last_in_{i}") for i in range(NTILE)]
        pair_ready, fsum_ready = sem("pair_ready"), sem("fsum_ready")
        frms_ready, fin_ready, fin_out = sem("frms_ready"), sem("fin_ready"), sem("fin_out")

        w_in = a["w_in"][0].rearrange("(c p) n -> p c n", p=P)
        w_out = a["w_out"][0].rearrange("(c p) n -> p c n", p=P)
        x_p, x_s = a["x_prompt"][0], a["x_sample"].rearrange("b t d -> (b t) d")
        cut = [0, 256, 512, 768, 1024, 1280, 1544, 1800, 2056]
        GATE_COL = 1536

        def x_rows(i):
            return x_p[i * P:(i + 1) * P, :] if i < NT else x_s

        def landed(k):
            return piece_in[k % RING], 16 * (k // RING + 1)

        def piece(k):
            return ring[:, k % RING, :]

        def slot_of(k):
            return (N_FIRST + k) % RING

        def rounded_r(k):
            return ring_r[:, RING + (N_FIRST + k) % HIS, :]

        def rest_r(k):
            return ring_r[:, slot_of(k), :]

        CONSTS = 6
        DEC_IN = 12

        TOK_AT = ZO + 2

        block = ctx.enter_context(nc.Block())

        def split(eng, k):
            w = ring[:, slot_of(k), :]
            return eng.tensor_tensor(rest_r(k), w, rounded_r(k).bitcast(F32), ALU.subtract)

        @block.sync
        def _(sp):
            def load_first(k):
                if k >= RING:
                    sp.wait_ge(pieces_used, k - RING + 1)
                if k < N_IN:
                    dst = piece(k).rearrange("p (c n) -> p c n", c=KC)
                    src = w_in[:, :, cut[k]:cut[k] + 256]
                else:
                    c = 2 * (k - N_IN)
                    dst = piece(k).rearrange("p (c n) -> p c n", c=2)
                    src = w_out[:, c:c + 2, :]
                sp.dma_start(dst, src).then_inc(landed(k)[0], 16)

            for i in range(NTILE):
                if i >= 2:
                    sp.wait_ge(xT_psum, 2 * (i - 1))
                    sp.wait_ge(rms_ready, i - 1)
                sp.dma_start(xbuf[0:rows(i), i % 2, :], x_rows(i)).then_inc(x_in[i % 2], 16)
                if i == 1:
                    for k in range(4):
                        load_first(k)
            for k in range(4, N_FIRST):
                load_first(k)

            def load_experts(base):
                with sp.Fori(0, NE // 2) as pair:
                    used = sp.snap(pair * (2 * N_PIECE) + base * N_PIECE)
                    for k in range(2 * N_PIECE):
                        m, q = k % N_PIECE // 4, k % 4
                        w = a[("w_gate", "w_up", "w_down")[m]][0].rearrange("e (c p) n -> p e c n", p=P)
                        if m == 1:
                            chunks, columns = slice(4 * (q % 2), 4 * (q % 2) + 4), slice(512 * (q // 2), 512 * (q // 2) + 512)
                        else:
                            chunks, columns = slice(2 * q, 2 * q + 2), slice(0, D)
                        alone(sp, pieces_used, used + (k + N_FIRST - RING + 1))
                        sp.dma_start(ring[:, slot_of(k), :].rearrange("p (c n) -> p c n", c=4 if m == 1 else 2),
                                     w[:, bass.ds(pair * 2 + k // N_PIECE, 1), chunks, columns
                                       ].rearrange("p e c n -> p (e c) n")).then_inc(piece_in[slot_of(k)], 16)

            load_experts(0)
            sp.wait_ge(count_ready, 1)
            most = sp.value_load(count_i[0:1, 0:1], min_val=0, max_val=TT)
            turns = sp.snap(count_passes(most) * NE)
            all_used, out_0, out_1 = sp.snap(turns * N_PIECE + N_FIRST), sp.snap(turns * 8), sp.snap(turns * 8 + 16)
            all_split = sp.snap(turns * N_PIECE + AHEAD)
            with sp.Fori(1, PASSES) as again:
                with sp.If(again * CAP < most):
                    load_experts(again * NE)
            for k in range(AHEAD):
                alone(sp, pieces_used, turns * N_PIECE + (k + N_FIRST - RING + 1))
                sp.dma_start(ring[:, slot_of(k), :].rearrange("p (c n) -> p c n", c=2),
                             a["w_gate"][0][0].rearrange("(c p) n -> p c n", p=P)[:, 2 * k:2 * k + 2, :]
                             ).then_inc(piece_in[slot_of(k)], 16)
            alone(sp, pieces_used, all_used)
            alone(sp, lo_ready, all_split)
            alone(sp, rows_out[0], out_0)
            alone(sp, rows_out[1], out_1)
            for i in FINAL:
                src = moe_rows[i * P * TOPK:(i * P + rows(i)) * TOPK, :].rearrange("(p k) n -> p (k n)", k=TOPK)
                sp.dma_start(y_all[0:rows(i), i, :], src).then_inc(last_in[i], 16)

        @block.gpsimd
        def _(pool):
            pool.memset(ident[:, :], 0.0)
            pool.drain()
            pool.affine_select(ident[:, :], ident[:, :], [[-1, P]], ALU.not_equal, 1.0, base=0,
                               channel_multiplier=1).then_inc(ident_made, 1)
            pool.memset(negsel[:, :], 0.0)
            pool.memset(v_tok[:, :, :, DV:DV + 1], 1.0)
            pool.memset(bias_rows, NEG)
            pool.drain()
            neg_v = negsel[:, :].rearrange("p (h n) -> p h n", h=MH)
            pool.affine_select(neg_v, neg_v, [[1, MH], [0, P]], ALU.not_equal, -1.0, base=0, channel_multiplier=-1)
            pool.wait_ge(relT_in, 16)
            starts = bucket_starts()
            for b in range(NBUCKET):
                lo, n = starts[b], starts[b + 1] - starts[b]
                pool.tensor_copy(bias_rows[:, 256 - lo - n:256 - lo], relT[:, b:b + 1].to_broadcast([AH, n]))
            pool.drain()
            pool.engine_nop().then_inc(rows_made, 1)

            for n in range(MH * NT):
                pool.wait_ge(wexp_ready, n + 1)
                w = wexp[:, n % 2, 0:P]
                pool.affine_select(w, w, [[1, P]], ALU.is_ge, 0.0, base=0,
                                   channel_multiplier=-1).then_inc(wmask_ready, 1)

            pool.wait_ge(state_psum, MH)
            pool.memset(g4, 1.0)
            pool.memset(r4, 1.0)
            pool.memset(r8, 0.0)
            pool.iota(kvi[:, 0:1], [[0, 1]], base=0, channel_multiplier=1)
            pool.memset(slot_dst[:, :].bitcast(I32), 2 * ROWS)
            pool.memset(slot_gate[:, :], 0.0)
            pool.drain()
            pool.affine_select(g4, g4, [[-4, 32]], ALU.is_ge, 0.0, base=0, channel_multiplier=1)
            pool.affine_select(r4, r4, [[1, P]], ALU.is_ge, 0.0, base=0, channel_multiplier=-4)
            r8v = r8.rearrange("p (b h) -> p b h", h=AH)
            pool.affine_select(r8v, r8v, [[0, NB], [1, AH]], ALU.not_equal, 1.0, base=0, channel_multiplier=-1)
            pool.tensor_copy(brow9[:, 0:129], bias_rows[:, 127:256])
            pool.drain()
            pool.affine_select(g4, g4, [[4, 32]], ALU.is_ge, 0.0, base=3, channel_multiplier=-1)
            pool.affine_select(r4, r4, [[-1, P]], ALU.is_ge, 0.0, base=3, channel_multiplier=4)
            pool.drain()
            pool.engine_nop().then_inc(masks_made, 1)

            for i in range(EARLY):
                pool.wait_ge(early_ready, i + 1)
                pool.wait_ge(xr_in[i], 16)
                pool.tensor_tensor(y1[:, i, :], y1[:, i, :], xbuf[:, i, :], ALU.add).then_inc(early_x, 1)

            pool.wait_ge(mixa_ready, NT)
            pool.wait_ge(pk_out, 32)
            pool.memset(route_v, 0.0)
            pool.memset(rank, -1.0)
            pool.memset(chosen, 0.0)
            pool.memset(tri, 1.0)
            pool.memset(ones, 1.0)
            pool.memset(id64, 0.0)
            pool.iota(iota_cap, [[1, CAP]], base=0, channel_multiplier=0, allow_small_or_imprecise_dtypes=True)
            pool.iota(iota_e, [[1, NE]], base=0, channel_multiplier=0, allow_small_or_imprecise_dtypes=True)
            pool.iota(tok_k, [[P * TOPK, NTILE], [1, TOPK]], base=1, channel_multiplier=TOPK,
                      allow_small_or_imprecise_dtypes=True)
            pool.drain()
            pool.affine_select(tri, tri, [[1, P]], ALU.is_gt, 0.0, base=0, channel_multiplier=-1)
            for base, cols_ in ((0, slice(0, NE)), (-NE, slice(0, NE + 1)), (0, slice(NE, NE + 1))):
                v = id64[:, cols_]
                pool.affine_select(v, v, [[-1, v.shape[1]]], ALU.not_equal, 1.0, base=base, channel_multiplier=1)
                pool.drain()
            pool.iota(route_v[:, :, :, 0], [[P, NTILE], [0, NE + 1]], base=0, channel_multiplier=1,
                      allow_small_or_imprecise_dtypes=True)
            pool.drain()
            pool.engine_nop().then_inc(iotas_made, 1)

            def gather(u, t1):
                alone(pool, slots_ready, t1)
                pool.indirect_dma_start(
                    xg[0:CAP, u, :], None, xhat_rows[:, :],
                    bass.IndirectOffsetOnAxis(slot_tok[0:CAP, u:u + 1], 0),
                    bounds_check=TT - 1, oob_is_err=False).then_inc(rows_in[u], 16)

            def scatter(u, t1):
                alone(pool, yrow_ready, t1)
                pool.indirect_dma_start(
                    moe_rows[:, :], bass.IndirectOffsetOnAxis(slot_dst[0:CAP, u:u + 1], 0),
                    yrow[0:CAP, u, :], None,
                    bounds_check=ROWS - 1, oob_is_err=False).then_inc(rows_out[u], 16)

            pool.wait_ge(xhat_out[0], 16 * 3)
            pool.wait_ge(xhat_out[1], 16 * 2)
            pool.wait_ge(count_ready, 1)
            most = pool.value_load(count_i[0:1, 0:1], min_val=0, max_val=TT)
            turns = pool.snap(count_passes(most) * NE)
            turns1 = pool.snap(turns + 1)
            gather(0, 1)
            with pool.Fori(0, PASSES) as again:
                with pool.If(again * CAP < most):
                    with pool.Fori(0, NE // 2) as pair:
                        t = [pool.snap(again * NE + pair * 2 + k) for k in range(4)]
                        for u in range(2):
                            scatter(1 - u, t[u + 1])
                            alone(pool, ex_psum, t[u])
                            gather(1 - u, t[u + 2])
            scatter(1, turns1)

            for i in FINAL:
                r = rows(i)
                pool.wait_ge(last_in[i], 16)
                pool.tensor_tensor(y_all[0:r, i, 2048:3072], y_all[0:r, i, 2048:3072], y_all[0:r, i, 3072:4096],
                                   ALU.add).then_inc(pair_ready, 1)

        @block.scalar
        def _(act):
            slow = dict(allow_slow_non_contiguous=True)

            def rms(col, n):
                act.drain()
                return act.activation(col, col, ACT.Sqrt, bias=eps_col[0:col.shape[0], :], scale=1.0 / n)

            act.dma_start(relT, a["rel_bias"].rearrange("b h -> h b"), **slow).then_inc(relT_in, 16)
            vec = reg_w[0:20, 0:P]
            act.dma_start(vec[0:8, :], a["norm1"][0].rearrange("(c p) -> c p", p=P)).then_inc(consts_in, 16)
            act.dma_start(reg_w[8:16, 0:P], a["norm2"][0].rearrange("(c p) -> c p", p=P)).then_inc(consts_in, 16)
            act.dma_start(reg_w[16:20, 0:P], a["m_gain"][0].rearrange("(c p) -> c p", p=P)).then_inc(consts_in, 16)
            act.dma_start(b_if, a["b_if"].rearrange("a n -> n a"), **slow).then_inc(consts_in, 16)
            act.dma_start(sink_bc, a["sinks"].to_broadcast([P, AH])).then_inc(consts_in, 16)
            act.dma_start(wif_v, w_in[:, :, GATE_COL:GATE_COL + 8]).then_inc(consts_in, 16)

            act.wait_ge(eps_made, 1)
            for i in range(NTILE):
                act.wait_ge(x_in[i % 2], 16 * (i // 2 + 1))
                act.activation(ring[0:rows(i), RING + HIS - 1, (i % 2) * D:(i % 2 + 1) * D], xbuf[0:rows(i), i % 2, :], ACT.Square,
                               accum_out=ssq[0:rows(i), i:i + 1])
                rms(ssq[0:rows(i), i:i + 1], D).then_inc(rms_ready, 1)
            act.dma_start(o["s_k"][0, :, 0:WIN - 1], a["cache_k"][0, :, 1:WIN]).then_inc(out_done, 16)
            act.dma_start(o["s_v"][0, :, 0:WIN - 1], a["cache_v"][0, :, 1:WIN]).then_inc(out_done, 16)
            act.wait_ge(rows_made, 1)
            act.dma_start(sc_bias.rearrange("h (q m) -> h q m", q=P),
                          bias_rows.unsqueeze(1).to_broadcast([AH, P, RLEN])).then_inc(bias_out, 16)

            tok_copies = ([(v_tok[:, i, :, 0:DV], 512) for i in range(NT)]
                          + [(k_tok[:, 2 * q:2 * q + 2, :], 512) for q in range(2)] + [(av_tok, 512), (ak_last, P)])

            def token_major(n):
                out, w = tok_copies[n]
                act.wait_ge(tok_psum, n + 1)
                src = ps[4 + 2 * (n % 2)][:, 0:w]
                if len(out.shape) == 3:
                    src = src.rearrange("p (a n) -> p a n", a=out.shape[1])
                act.activation(out, src, ACT.Copy).then_inc(tok_ready, 1)

            act.wait_ge(consts_in, 16 * CONSTS)

            def round_w_in(k):
                act.wait_ge(*landed(k))
                if k >= HIS:
                    act.wait_ge(pieces_used, k - HIS + 1)
                act.activation(rounded_r(k - N_FIRST), piece(k), ACT.Copy).then_inc(w_hi, 1)

            act.activation(wif_r[:, 0], wif_v, ACT.Copy).then_inc(w_hi, 1)
            round_w_in(0)
            round_w_in(1)
            for j in range(NZ + 1):
                if j % 2 == 0 and j // 2 + 2 < N_IN:
                    round_w_in(j // 2 + 2)
                if j == 4:
                    act.wait_ge(*absf_ready)
                    act.activation(g_rows[1][0:4, :], g_rows[1][0:4, :], ACT.Exp, scale=-1.0)
                    act.drain()
                    act.activation(g_rows[1][0:4, :], g_rows[1][0:4, :], ACT.Ln, bias=1.0).then_inc(lnf_ready, 1)
                if TOK_AT < j <= TOK_AT + 6:
                    token_major(j - TOK_AT - 1)
                act.wait_ge(proj_psum, j + 1)
                pair = 2 * (j % 2)
                for half in range(2):
                    cs = slice(half * HALF, (half + 1) * HALF)
                    if j == 0:
                        last = act.activation(gates[:, cs], ps[pair + half][0:8, 0:HALF], ACT.Identity, bias=b_if)
                    else:
                        b = j - 1
                        f = ACT.Sigmoid if ZO <= b < ZAQ else ACT.Copy
                        sc = DK ** -0.5 if ZK <= b < ZV else 1.0
                        last = act.activation(zT[:, b, cs], ps[pair + half][:, 0:HALF], f, scale=sc)
                last.then_inc(proj_ready, 1)

            act.dma_start(cache_ks, a["cache_k"][0].rearrange("b s g d -> s b (g d)")).then_inc(cache_in, 16)
            act.dma_start(cache_vs, a["cache_v"][0].rearrange("b s g d -> s b (g d)")).then_inc(cache_in, 16)
            act.drain()
            for n in range(4):
                act.wait_ge(zs_psum, n + 1)
                w = 512 if n < 3 else 264
                act.activation(zs[:, n * 512:n * 512 + w], ps[n % 2][0:NB, 0:w], ACT.Copy).then_inc(zs_ready, 1)
            act.wait_ge(zs_ready, 4)
            act.dma_start(sc_q[:, :], zs[:, 0:256]).then_inc(zs_out, 16)
            act.dma_start(sc_k[:, :], zs[:, 256:512]).then_inc(zs_out, 16)
            act.dma_start(sc_v[:, :], zs[:, 512:1024]).then_inc(zs_out, 16)
            act.dma_start(sc_aq[:, :], zs[:, 1024:1536]).then_inc(zs_out, 16)
            act.dma_start(sc_kv[0], zs[:, 1536:1664]).then_inc(zs_out, 16)
            act.dma_start(sc_kv[1], zs[:, 1664:1792]).then_inc(zs_out, 16)
            act.dma_start(sc_gate[0], zs[:, 1792:1796]).then_inc(zs_out, 16)
            act.dma_start(sc_gate[1], zs[:, 1796:1800]).then_inc(zs_out, 16)
            act.dma_start(o["s_k"][0, :, WIN - 1].rearrange("b g d -> b (g d)"), zs[:, 1536:1664]).then_inc(zs_out, 16)
            act.dma_start(o["s_v"][0, :, WIN - 1].rearrange("b g d -> b (g d)"), zs[:, 1664:1792]).then_inc(zs_out, 16)
            act.dma_start(ak_swap[0:64, :], zT[64:128, ZAK, 0:T]).then_inc(aksw_in, 16)
            act.dma_start(ak_swap[64:128, :], zT[0:64, ZAK, 0:T]).then_inc(aksw_in, 16)

            token_major(6)
            token_major(7)
            act.wait_ge(tok_ready, 8)
            act.dma_start(o["p_k"][0, 0].rearrange("s g d -> s (g d)"), ak_last).then_inc(pk_out, 16)
            act.dma_start(o["p_v"][0, 0].rearrange("s g d -> s (g d)"), av_tok[:, NT - 1, :]).then_inc(pk_out, 16)
            act.dma_start(c_state, a["state_C"][0].rearrange("b h (a k) v -> (b h a) (k v)", a=4)).then_inc(dec_in, 16)

            act.wait_ge(*grows_ready)
            act.dma_start(o["p_m"][0].rearrange("a h -> h a"), gsc[0:4, 20:21], **slow).then_inc(state_out, 16)
            act.wait_ge(*gtok_ready)

            act.activation(exp_m, nm_tok, ACT.Exp).then_inc(expm_ready, 1)
            n = 0
            for h in range(MH):
                act.wait_ge(negm_psum, h + 1)
                act.wait_ge(wpre_ready, NT * h)
                act.wait_ge(kg_ready, h)
                act.activation(neg_m, ps[0][:, :], ACT.Copy)
                act.drain()
                act.activation(gsc[:, 0:4], u_tok[:, :, h], ACT.Exp, bias=neg_m[:, T - 1:T]).then_inc(gs_ready, 1)
                for kb in range(NT):
                    n += 1
                    act.wait_ge(wpre_ready, n)
                    w = wexp[:, (n - 1) % 2, 0:T - kb * P]
                    act.activation(w, w, ACT.Exp).then_inc(wexp_ready, 1)
            act.wait_ge(hss_ready, 1)
            rms(h_ss, DV).then_inc(hrms_ready, 1)
            act.wait_ge(state_psum, MH)
            act.wait_ge(zs_out, 16 * 10)
            act.dma_start(n16, a["state_n"][0].rearrange("b h (a k) -> (b h a) k", k=16)).then_inc(dec_in, 16)
            act.dma_start(q16, sc_q.rearrange("b (a k) -> (b a) k", k=16)).then_inc(dec_in, 16)
            act.dma_start(k16, sc_k.rearrange("b (a k) -> (b a) k", k=16)).then_inc(dec_in, 16)
            act.dma_start(r32[:, 0:P], sc_v.rearrange("b (h n) -> (b h) n", h=MH)).then_inc(dec_in, 16)
            act.dma_start(q64, sc_aq.rearrange("b (h n) -> (b h) n", h=AH)).then_inc(dec_in, 16)
            act.dma_start(kv16[:, 0:64], sc_kv[0].rearrange("b (g n) -> (b g) n", g=KV)).then_inc(dec_in, 16)
            act.dma_start(kv16[:, 64:128], sc_kv[1].rearrange("b (g n) -> (b g) n", g=KV)).then_inc(dec_in, 16)
            for c in range(2):
                act.dma_start(gpre[:, c:c + 1], sc_gate[c].rearrange("b (h a) -> (b h) a", a=1), **slow).then_inc(dec_in, 16)
            act.dma_start(m32, a["state_m"][0].rearrange("b (h a) -> (b h) a", a=1), **slow).then_inc(dec_in, 16)
            act.wait_ge(masks_made, 1)
            act.dma_start(brow9[:, 129:130], a["sinks"].rearrange("a h -> h a"), **slow).then_inc(dec_in, 16)
            act.wait_ge(state_ready, MH)
            states = reg_x[0:DK, 0:MH * (DV + 1)].rearrange("k (h v) -> k h v", h=MH)
            act.dma_start(o["p_C"][0, 0].rearrange("h k v -> k h v"), states[:, :, 0:DV]).then_inc(state_out, 16)
            act.dma_start(o["p_n"][0, 0].rearrange("h k -> k h").unsqueeze(2), states[:, :, DV:DV + 1],
                          **slow).then_inc(state_out, 16)

            act.wait_ge(mixm_ready, MH)
            act.wait_ge(bias_out, 16)
            skew = bass.AP(sc_bias.tensor, P - 1, [[RLEN - 1, P], [P * RLEN, AH], [1, 2 * P]])
            act.dma_start(bias, skew).then_inc(bias_in, 16)

            def early_share(i):
                act.wait_ge(early_psum, i + 1)
                for q in range(2):
                    last = act.activation(y1[:, i, 512 * q:512 * q + 512], ps[q][:, :], ACT.Copy)
                last.then_inc(early_ready, 1)

            act.wait_ge(*dabs_ready)
            act.activation(d32[:, 1:2], d32[:, 0:1], ACT.Exp, scale=-1.0)
            act.drain()
            act.activation(d32[:, 2:3], d32[:, 1:2], ACT.Ln, bias=1.0).then_inc(sample_act, 1)
            early_share(0)
            act.wait_ge(*dm_ready)
            act.activation(r32[:, 128:129], d32[:, 4:5], ACT.Exp, bias=d32[:, 6:7])
            act.activation(r32[:, 129:130], gpre[:, 0:1], ACT.Exp, bias=d32[:, 6:7])
            act.activation(d32[:, 7:8], d32[:, 6:7], ACT.Exp).then_inc(sample_act, 1)
            act.wait_ge(*rep_psum)
            act.activation(vrep[:, 0:130], ps[4][:, 0:130], ACT.Copy).then_inc(sample_act, 1)
            act.wait_ge(*dstate_ready)
            act.dma_start(o["s_C"][0].rearrange("b h (a k) v -> (b h a) (k v)", a=4), c_state).then_inc(dstate_out, 16)
            act.dma_start(o["s_n"][0].rearrange("b h (a k) -> (b h a) k", k=16), n16).then_inc(dstate_out, 16)
            act.dma_start(o["s_m"][0].rearrange("b (h a) -> (b h) a", a=1), d32[:, 5:6], **slow).then_inc(dstate_out, 16)
            act.wait_ge(*dss_ready)
            rms(d32[:, 10:11], DV).then_inc(drms_ready, 1)
            act.wait_ge(*dh_ready)
            act.dma_start(sc_mix[0].rearrange("b (h n) -> (b h) n", h=MH), h32).then_inc(mixs_out, 16)
            early_share(1)
            for b in range(NB):
                act.wait_ge(kc_psum, b + 1)
                if b >= 2:
                    act.wait_ge(ks_psum, b - 1)
                act.activation(kT_s[:, b % 2, :], ps[4 + 2 * (b % 2)][:, 0:P], ACT.Copy).then_inc(kc_ready, 1)
            act.wait_ge(ks_psum, NB)
            act.activation(sT, ps[7][:, 0:64], ACT.Copy).then_inc(sample_act, 1)
            act.wait_ge(*dlogit_ready)
            act.activation(dl[:, 0:129], dl[:, 0:129], ACT.Exp, bias=ds[:, 1:2], accum_out=ds[:, 2:3])
            act.activation(ds[:, 3:4], ds[:, 5:6], ACT.Exp, bias=ds[:, 1:2]).then_inc(sample_act, 1)
            act.wait_ge(*dpT_psum)
            act.activation(pT, ps[5][:, 256:320], ACT.Copy).then_inc(sample_act, 1)
            act.wait_ge(*do_psum)
            act.activation(oT, ps[6][:, 256:320], ACT.Copy).then_inc(sample_act, 1)
            act.wait_ge(*datt_ready)
            act.dma_start(sc_mix[1].rearrange("b (h n) -> (b h) n", h=AH), a64).then_inc(mixs_out, 16)
            act.wait_ge(mixs_out, 32)
            act.wait_ge(dstate_out, 48)
            for i in range(2):
                act.dma_start(xbuf[0:rows(i), i, :], x_rows(i)).then_inc(xr_in[i], 16)
            act.dma_start(mix_s.rearrange("b (c n) -> b c n", c=2), sc_mix.rearrange("c b n -> b c n")
                          ).then_inc(mixs_in, 16)

            def load_bias(m):
                for half in range(2):
                    act.dma_start(e_bias[m][32 * half:32 * half + 32, :], a[("b_gate", "b_up", "b_down")[m]][0]
                                  ).then_inc(bias_rows_in, 16)

            load_bias(1)
            load_bias(2)

            def evac_pT(n):
                c, lo = (n - 1) % 2, P if n <= AH else 0
                act.wait_ge(pT_psum, n)
                if n > 2:
                    act.wait_ge(pv_psum, n - 2)
                act.activation(probT[:, c, lo:], ps[2 + c][:, lo:256], ACT.Copy).then_inc(pT_ready, 1)

            for n in range(1, NT * AH + 1):
                i, h = divmod(n - 1, AH)
                c, lo = (n - 1) % 2, P if i == 0 else 0
                act.wait_ge(logit_ready, n)
                act.activation(prob[:, c, lo:], prob[:, c, lo:], ACT.Exp,
                               bias=nmax[:, h:h + 1], accum_out=asum[:, h:h + 1]).then_inc(prob_ready, 1)
                if h:
                    evac_pT(n - 1)
                if h == AH - 1:
                    evac_pT(n)
                    act.wait_ge(sinkin_ready, i + 1)
                    act.activation(asnk, asnk, ACT.Exp).then_inc(sinkexp_ready, 1)

            act.wait_ge(mixa_ready, NT)
            act.wait_ge(mixs_ready, 1)
            act.wait_ge(pk_out, 32)
            load_bias(0)
            act.dma_start(n2_bc, a["norm2"].to_broadcast([P, D])).then_inc(late_in, 16)
            act.dma_start(w_rt, a["w_router"][0].rearrange("(c p) e -> p c e", p=P)).then_inc(late_in, 16)
            act.dma_start(br_bc, a["b_router"].to_broadcast([P, NE])).then_inc(late_in, 16)
            act.dma_start(fn_bc, a["final_norm"].rearrange("(a n) -> a n", a=1).to_broadcast([P, D])).then_inc(late_in, 16)
            act.wait_ge(bias_rows_in, 16 * 6)
            for m in range(3):
                if m == 2:
                    act.wait_ge(bias_lo, 1)
                act.activation(e_bias_tmp_r[m], e_bias[m][32:64, :], ACT.Copy)
                act.activation(e_bias_r[m][0:32, :], e_bias[m][0:32, :], ACT.Copy).then_inc(bias_hi, 1)

            for i in range(NTILE):
                r = rows(i)
                act.wait_ge(y_ready, i + 1)
                if i + 2 < NTILE:
                    act.dma_start(xbuf[0:rows(i + 2), i % 2, :], x_rows(i + 2)).then_inc(xr_in[i % 2], 16)
                act.drain()
                if i == 2:
                    act.wait_ge(bias_lo, 3)
                act.activation(junk[0:r, :], y1[0:r, i, :], ACT.Square, accum_out=ssq[0:r, i:i + 1])
                rms(ssq[0:r, i:i + 1], D).then_inc(rms2_ready, 1)
                act.wait_ge(xhat_ready, i + 1)
                act.dma_start(xhat_rows[i * P:i * P + r, :], xhat[0:r, i % 2, :]).then_inc(xhat_out[i % 2], 16)
                act.wait_ge(top_ready, i + 1)
                act.activation(gexp[0:r, :], top8[0:r, 0:4], ACT.Exp, bias=rs1[0:r, 0:1],
                               accum_out=rs1[0:r, 1:2]).then_inc(gexp_ready, 1)

            def round_piece(k, p12, p48):
                g = N_FIRST + k
                act.wait_ge(piece_in[slot_of(k)], p48 + 16 * (g // RING + 1))
                act.wait_ge(pieces_used, p12 + (g - HIS + 1))
                act.activation(rounded_r(k), ring[:, slot_of(k), :], ACT.Copy).then_inc(hi_ready, 1)

            for k in range(AHEAD):
                round_piece(k, 0, 0)
            act.wait_ge(count_ready, 1)
            most = act.value_load(count_i[0:1, 0:1], min_val=0, max_val=TT)
            turns = act.snap(count_passes(most) * NE)

            def rows_of(u, t, used):
                act.wait_ge(slots_ready, t + 1)
                act.wait_ge(pieces_used, used)
                for q in range(2):
                    last = act.activation(yrow[0:CAP, u, 512 * q:512 * q + 512], ps[4 + q][0:CAP, :], ACT.Copy,
                                          scale=slot_gate[0:CAP, u:u + 1])
                last.then_inc(yrow_ready, 1)

            def round_blocks(out, bank, q0, q1):
                for q in range(q0, q1):
                    last = act.activation(out[:, 0, 4 * q:4 * q + 4, :],
                                          ps[bank + q][:, 0:4 * CAP].rearrange("p (c n) -> p c n", c=4), ACT.Copy)
                return last

            act.wait_ge(ex_psum, 1)
            round_blocks(eX, 6, 0, 2).then_inc(xhi_ready, 1)
            with act.Fori(0, PASSES) as again:
                with act.If(again * CAP < most):
                    with act.Fori(0, NE // 2) as pair:
                        t0 = act.snap(again * NE + pair * 2)
                        p12, p48 = act.snap(t0 * N_PIECE), act.snap(t0 * 24)
                        for u in range(2):
                            k = N_PIECE * u
                            rows_of(1 - u, t0 + u, p12 + (k + N_FIRST))
                            for n in range(3, 8):
                                round_piece(k + n, p12, p48)
                            act.wait_ge(g_ready, t0 + u + 1)
                            act.activation(eS[0:CAP, :], eG[0:CAP, :], ACT.Sigmoid, scale=ALPHA).then_inc(sg_ready, 1)
                            for n in range(8, 11):
                                round_piece(k + n, p12, p48)
                            act.wait_ge(hT_psum2, t0 * 2 + (2 * u + 1))
                            round_blocks(eH, 0, 0, 1).then_inc(hhi_ready, 1)
                            round_piece(k + 11, p12, p48)
                            act.wait_ge(ex_psum, t0 + u + 2)
                            round_blocks(eX, 6, 0, 2).then_inc(xhi_ready, 1)
                            act.wait_ge(hT_psum2, t0 * 2 + (2 * u + 2))
                            round_blocks(eH, 0, 1, 2).then_inc(hhi_ready, 1)
                            for n in range(12, 15):
                                round_piece(k + n, p12, p48)
            rows_of(1, turns, turns * N_PIECE + N_FIRST)

            def store(n):
                i = FINAL[n]
                act.wait_ge(fin_ready, n + 1)
                dst = o["y_prompt"][0, i * P:(i + 1) * P, :] if i < NT else o["y_sample"].rearrange("b t d -> (b t) d")
                act.dma_start(dst, y1[0:rows(i), i, :]).then_inc(fin_out, 16)

            for n, i in enumerate(FINAL):
                r = rows(i)
                act.wait_ge(fsum_ready, n + 1)
                act.activation(y_all[0:r, i, 2048:3072], y1[0:r, i, :], ACT.Square, accum_out=ssq[0:r, i:i + 1])
                rms(ssq[0:r, i:i + 1], D).then_inc(frms_ready, 1)
                if n:
                    store(n - 1)
            store(NTILE - 1)
            act.wait_ge(fin_out, 16 * NTILE)
            act.wait_ge(out_done, 16 * 2)
            act.wait_ge(state_out, 16 * 3)

        @block.vector
        def _(dve):
            dve.memset(eps_col, EPS).then_inc(eps_made, 1)
            dve.wait_ge(*cols_psum)
            dve.tensor_copy(cols[:, :], ps[6][:, 0:20])
            dve.drain()

            def norm_rows(i):
                r = rows(i)
                dve.wait_ge(rms_ready, i + 1)
                dve.reciprocal(ssq[0:r, i:i + 1], ssq[0:r, i:i + 1])
                dve.drain()
                dve.tensor_scalar(xbuf[0:r, i % 2, :], xbuf[0:r, i % 2, :], ssq[0:r, i:i + 1], None,
                                  ALU.mult).then_inc(xn_ready, 1)

            def evac_xT(i):
                r = rows(i)
                for q in range(2):
                    n = 2 * i + q
                    dve.wait_ge(xT_psum, n + 1)
                    dve.tensor_tensor(xnT_hi[:, 4 * q:4 * q + 4, i * P:i * P + r],
                                      ps[4 + q][:, 0:4 * P].rearrange("p (c t) -> p c t", c=4)[:, :, 0:r],
                                      cols[:, 4 * q:4 * q + 4].unsqueeze(2).to_broadcast([P, 4, r]), ALU.mult)
                    dve.drain()
                    for c in range(4):
                        k = 4 * q + c
                        last = dve.scalar_tensor_tensor(xnT_lo[k][:, i * P:i * P + r], ps[4 + q][:, c * P:c * P + r],
                                                        cols[:, k:k + 1], xnT_hi[:, k, i * P:i * P + r].bitcast(F32), ALU.mult,
                                                        ALU.subtract)
                    last.then_inc(xT_ready, 1)

            def rest_of_w_in(k):
                dve.wait_ge(w_hi, k + 2)
                dve.tensor_tensor(rest_r(k - N_FIRST), piece(k), rounded_r(k - N_FIRST).bitcast(F32), ALU.subtract).then_inc(w_lo, 1)

            for i in range(NTILE + 1):
                if i < NTILE:
                    norm_rows(i)
                else:
                    dve.wait_ge(w_hi, 1)
                    dve.tensor_tensor(wif_r[:, 1], wif_v, wif_r[:, 0].bitcast(F32), ALU.subtract).then_inc(w_lo, 1)
                    rest_of_w_in(0)
                if i:
                    evac_xT(i - 1)

            f_row, l_row, z_row, lf_row = (g[0:4, :] for g in g_rows)
            rest_of_w_in(1)
            rest_of_w_in(2)
            dve.wait_ge(*f_psum)
            f_ps = ps[6][0:4, :]
            dve.tensor_copy(f_row, f_ps)
            dve.memset(z_row, 0.0)
            dve.drain()
            dve.scalar_tensor_tensor(l_row, f_row, -1.0, f_row, ALU.mult, ALU.max).then_inc(gate_dve, 1)
            rest_of_w_in(3)
            dve.wait_ge(lnf_ready, 1)
            dve.drain()
            dve.scalar_tensor_tensor(lf_row, f_row, 0.0, l_row, ALU.min, ALU.subtract)
            dve.drain()
            b_row, u_row, nm_row, m_row = f_row, l_row, lf_row, gates[0:4, 0:T]
            dve.tensor_tensor_scan(b_row, lf_row, z_row, 0.0, ALU.add, ALU.add)
            dve.drain()
            dve.tensor_tensor(u_row, gates[0:4, 0:T], b_row, ALU.subtract)
            dve.drain()
            dve.tensor_tensor_scan(m_row, u_row, u_row, 0.0, ALU.max, ALU.max)
            dve.drain()
            dve.scalar_tensor_tensor(nm_row, b_row, -1.0, m_row, ALU.mult, ALU.subtract)
            dve.drain()
            dve.tensor_scalar(gsc[0:4, 20:21], nm_row[:, T - 1:T], -1.0, None, ALU.mult).then_inc(gate_dve, 1)
            for k in range(4, N_IN):
                rest_of_w_in(k)
            dve.wait_ge(*gtok_psum)
            dve.tensor_copy(small[:, 56:88], ps[5][:, 0:32]).then_inc(gate_dve, 1)
            dve.drain()

            def weights(h, kb, n):
                if n > 2:
                    dve.wait_ge(num_kb, n - 2)
                w = wexp[:, (n - 1) % 2, 0:T - kb * P]
                dve.tensor_scalar(w, neg_m[:, kb * P:T], u_tok[:, kb, h:h + 1], 0.0, ALU.add,
                                  ALU.min).then_inc(wpre_ready, 1)

            dve.wait_ge(zs_out, 16 * 10)
            dve.wait_ge(gs_ready, 1)
            weights(0, 0, 1)
            for h in range(MH):
                dve.wait_ge(state_psum, h)
                dve.tensor_tensor(kg, k_tok[:, :, h * DK:(h + 1) * DK],
                                  gsc[:, 0:4].unsqueeze(2).to_broadcast([P, NT, DK]), ALU.mult).then_inc(kg_ready, 1)
                for kb in range(NT):
                    n = NT * h + kb + 1
                    if kb + 1 < NT:
                        weights(h, kb + 1, n + 1)
                    dve.wait_ge(wmask_ready, n)
                    dve.wait_ge(score_psum, n)
                    w = wexp[:, (n - 1) % 2, 0:T - kb * P]
                    dve.tensor_tensor(w, w, ps[4 + (n - 1) % 2][:, 0:T - kb * P], ALU.mult).then_inc(wgt_ready, 1)
                if h + 1 < MH:
                    dve.wait_ge(gs_ready, h + 2)
                    weights(h + 1, 0, NT * (h + 1) + 1)
                dve.wait_ge(num_psum, h + 1)
                dve.wait_ge(expm_ready, 1)
                num = [ps[6 + q][:, 0:2 * (DV + 1)].rearrange("p (i n) -> p i n", i=2) for q in range(2)]
                den = gsc[:, 8:12]
                for q in range(2):
                    dve.tensor_copy(den[:, 2 * q:2 * q + 2].unsqueeze(2), num[q][:, :, DV:DV + 1])
                dve.drain()
                dve.scalar_tensor_tensor(den, den, -1.0, den, ALU.mult, ALU.max)
                dve.drain()
                dve.tensor_tensor(den, den, exp_m[:, :, h], ALU.max)
                dve.drain()
                dve.reciprocal(den, den)
                dve.drain()
                hv = h_rows[h].rearrange("p (i n) -> p i n", i=NT)
                for q in range(2):
                    last = dve.tensor_tensor(hv[:, 2 * q:2 * q + 2, :], num[q][:, :, 0:DV],
                                             den[:, 2 * q:2 * q + 2].unsqueeze(2).to_broadcast([P, 2, DV]), ALU.mult)
                last.then_inc(num_used, 1)
                dve.drain()
                dve.tensor_tensor(h_sq, hv, hv, ALU.mult)
                dve.drain()
                last = dve.tensor_reduce(h_ss[:, NT * h:NT * h + NT], h_sq, AX_X, ALU.add)
                if h == MH - 1:
                    last.then_inc(hss_ready, 1)
                dve.wait_ge(state_psum, h + 1)
                dve.tensor_copy(h_state[h], ps[1][0:DK, 0:DV + 1]).then_inc(state_ready, 1)
            dve.wait_ge(hrms_ready, 1)
            dve.reciprocal(h_ss, h_ss)
            dve.drain()
            for h in range(MH):
                hv = h_rows[h].rearrange("p (i n) -> p i n", i=NT)
                dve.tensor_tensor(hv, hv, h_ss[:, NT * h:NT * h + NT].unsqueeze(2).to_broadcast([P, NT, DV]),
                                  ALU.mult).then_inc(hn_ready, 1)
            for h in range(MH):
                dve.wait_ge(hT_psum, h + 1)
                dve.scalar_tensor_tensor(mixT[:, h, 0:T], ps[2 + h % 2][:, :], cols[:, 16 + h:17 + h], zT[:, ZO + h, 0:T],
                                         ALU.mult, ALU.mult).then_inc(mixm_ready, 1)

            dve.wait_ge(dec_in, 16 * DEC_IN)
            dve.wait_ge(consts_in, 16 * CONSTS)
            dve.wait_ge(masks_made, 1)
            dve.wait_ge(state_out, 16 * 3)
            dve.scalar_tensor_tensor(d32[:, 0:1], gpre[:, 1:2], -1.0, gpre[:, 1:2], ALU.mult, ALU.max).then_inc(sample_dve, 1)
            dve.tensor_scalar(kvi[:, 1:2], kvi[:, 0:1], 4, None, ALU.bitwise_and)
            dve.drain()
            dve.tensor_copy(kvm[:, 1:2], kvi[:, 1:2])
            dve.drain()
            dve.tensor_scalar(kvm[:, 1:2], kvm[:, 1:2], 0.25, None, ALU.mult)
            dve.drain()
            dve.tensor_scalar(kvm[:, 0:1], kvm[:, 1:2], -1.0, 1.0, ALU.mult, ALU.add)
            dve.drain()
            for g in range(KV):
                last = dve.tensor_scalar(q2[:, g * HD:(g + 1) * HD], q64, kvm[:, g:g + 1], None, ALU.mult)
            last.then_inc(sample_dve, 1)
            c_v = c_state.rearrange("p (k v) -> p k v", k=16)
            p_v = c_prod.rearrange("p (k v) -> p k v", k=16)
            dve.tensor_tensor(p_v, c_v, q16.unsqueeze(2).to_broadcast([P, 16, DV]), ALU.mult)
            dve.tensor_tensor(kw16, q16, k16, ALU.mult)
            dve.drain()
            dve.tensor_reduce(part[:, 0:DV], c_prod.rearrange("p (k v) -> p v k", k=16), AX_X, ALU.add)
            dve.tensor_reduce(part[:, DV:DV + 1], kw16, AX_X, ALU.add)
            dve.drain()
            dve.tensor_tensor(kw16, q16, n16, ALU.mult)
            dve.drain()
            dve.tensor_reduce(part[:, DV + 1:DV + 2], kw16, AX_X, ALU.add).then_inc(sample_dve, 1)
            dve.wait_ge(*dln_ready)
            dve.scalar_tensor_tensor(d32[:, 3:4], gpre[:, 1:2], 0.0, d32[:, 2:3], ALU.min, ALU.subtract)
            dve.drain()
            dve.tensor_tensor(d32[:, 4:5], d32[:, 3:4], m32, ALU.add)
            dve.drain()
            dve.tensor_tensor(d32[:, 5:6], d32[:, 4:5], gpre[:, 0:1], ALU.max)
            dve.drain()
            dve.tensor_scalar(d32[:, 6:7], d32[:, 5:6], -1.0, None, ALU.mult).then_inc(sample_dve, 1)
            dve.wait_ge(*vrep_ready)
            dve.tensor_scalar(kw16, k16, vrep[:, 129:130], None, ALU.mult)
            dve.drain()
            dve.tensor_tensor(p_v, kw16.unsqueeze(2).to_broadcast([P, 16, DV]),
                              vrep[:, 0:DV].unsqueeze(1).to_broadcast([P, 16, DV]), ALU.mult)
            dve.scalar_tensor_tensor(n16, n16, vrep[:, 128:129], kw16, ALU.mult, ALU.add)
            dve.drain()
            dve.scalar_tensor_tensor(c_state, c_state, vrep[:, 128:129], c_prod, ALU.mult,
                                     ALU.add).then_inc(sample_dve, 1)
            dve.wait_ge(*dsum_psum)
            we, wi = r32[:, 128:129], r32[:, 129:130]
            dve.tensor_tensor(d32[:, 8:9], ps[5][0:32, DV:DV + 1], wi, ALU.mult)
            dve.drain()
            dve.tensor_scalar(s32, r32[:, 0:DV], d32[:, 8:9], None, ALU.mult)
            dve.tensor_scalar(d32[:, 9:10], ps[5][0:32, DV + 1:DV + 2], we, d32[:, 8:9], ALU.mult, ALU.add)
            dve.drain()
            dve.scalar_tensor_tensor(h32, ps[5][0:32, 0:DV], we, s32, ALU.mult, ALU.add)
            dve.scalar_tensor_tensor(d32[:, 9:10], d32[:, 9:10], -1.0, d32[:, 9:10], ALU.mult, ALU.max)
            dve.drain()
            dve.tensor_tensor(d32[:, 9:10], d32[:, 9:10], d32[:, 7:8], ALU.max)
            dve.drain()
            dve.reciprocal(d32[:, 9:10], d32[:, 9:10])
            dve.drain()
            dve.tensor_scalar(h32, h32, d32[:, 9:10], None, ALU.mult)
            dve.drain()
            dve.tensor_tensor(s32, h32, h32, ALU.mult)
            dve.drain()
            dve.tensor_reduce(d32[:, 10:11], s32, AX_X, ALU.add).then_inc(sample_dve, 1)
            dve.wait_ge(drms_ready, 1)
            dve.reciprocal(d32[:, 10:11], d32[:, 10:11])
            dve.drain()
            dve.tensor_scalar(h32, h32, d32[:, 10:11], None, ALU.mult).then_inc(sample_dve, 1)

            dve.wait_ge(*own_psum)
            dve.tensor_copy(qbd, ps[3][:, 384:448]).then_inc(sample_dve, 1)
            dve.tensor_copy(kvown, ps[3][0:64, 256:384])
            dve.tensor_copy(ds[:, 5:6], ps[3][0:64, 129:130])
            dve.drain()
            dve.tensor_tensor(o64[:, 0:HD], q64, kvown[:, 0:HD], ALU.mult)
            dve.drain()
            dve.tensor_reduce(ds[:, 4:5], o64[:, 0:HD], AX_X, ALU.add)
            dve.drain()
            dve.scalar_tensor_tensor(dl[:, 128:129], ds[:, 4:5], HD ** -0.5, ps[3][0:64, 128:129], ALU.mult, ALU.add)
            dve.tensor_copy(o64, ps[3][0:64, 0:P])
            dve.drain()
            dve.wait_ge(*srow_psum)
            dve.scalar_tensor_tensor(dl[:, 0:P], ps[5][0:64, 0:P], HD ** -0.5, o64, ALU.mult, ALU.add)
            dve.drain()
            dve.tensor_reduce(ds[:, 0:1], dl[:, 0:129], AX_X, ALU.max)
            dve.drain()
            dve.tensor_scalar(ds[:, 1:2], ds[:, 0:1], ds[:, 5:6], -1.0, ALU.max, ALU.mult).then_inc(sample_dve, 1)
            dve.wait_ge(*dprob_ready)
            dve.tensor_tensor(ds[:, 6:7], ds[:, 2:3], ds[:, 3:4], ALU.add)
            dve.drain()
            dve.reciprocal(ds[:, 6:7], ds[:, 6:7])
            dve.tensor_scalar(a64, kvown[:, HD:P], dl[:, 128:129], None, ALU.mult)
            dve.drain()
            dve.wait_ge(*orow_psum)
            for g in range(KV):
                dve.scalar_tensor_tensor(a64, ps[7][0:64, P + g * HD:P + (g + 1) * HD], kvm[:, g:g + 1], a64,
                                         ALU.mult, ALU.add)
                dve.drain()
            dve.tensor_scalar(a64, a64, ds[:, 6:7], None, ALU.mult).then_inc(sample_dve, 1)

            dve.wait_ge(bias_in, 16)
            dve.wait_ge(bias_out, 16)
            n = 0
            for i in range(NT):
                lo = P if i == 0 else 0
                for h in range(AH):
                    n += 1
                    c = (n - 1) % 2
                    dve.wait_ge(s_psum, n)
                    if n > 2:
                        dve.wait_ge(pT_psum, n - 2)
                    p_ = prob[:, c, lo:]
                    dve.scalar_tensor_tensor(p_, ps[4 + c][:, lo:256], HD ** -0.5, bias[:, h, lo:],
                                             ALU.mult, ALU.add)
                    dve.drain()
                    dve.tensor_reduce(amax[:, h:h + 1], p_, AX_X, ALU.max)
                    dve.drain()
                    dve.tensor_scalar(nmax[:, h:h + 1], amax[:, h:h + 1], sink_bc[:, h:h + 1], -1.0, ALU.max,
                                      ALU.mult).then_inc(logit_ready, 1)
                dve.drain()
                dve.tensor_tensor(asnk, sink_bc, nmax, ALU.add).then_inc(sinkin_ready, 1)
                dve.wait_ge(sinkexp_ready, i + 1)
                dve.tensor_tensor(asnk, asnk, asum, ALU.add)
                dve.drain()
                dve.reciprocal(asnk, asnk)
                dve.drain()
                dve.wait_ge(pv_psum, AH * (i + 1))
                dve.wait_ge(oT_psum, i)
                dve.tensor_tensor(o_tok.rearrange("p (h n) -> p h n", h=AH),
                                  ps[6 + i % 2][:, :].rearrange("p (h n) -> p h n", h=AH),
                                  asnk.unsqueeze(2).to_broadcast([P, AH, HD]), ALU.mult).then_inc(otok_ready, 1)
                dve.wait_ge(oT_psum, i + 1)
                dve.tensor_copy(mixT[:, 4:8, i * P:(i + 1) * P],
                                ps[i % 2][:, :].rearrange("p (c t) -> p c t", c=4)).then_inc(mixa_ready, 1)
            dve.wait_ge(mixs_psum, 1)
            m_ps = ps[3][:, 0:8 * NB].rearrange("p (c t) -> p c t", c=KC)
            for h in range(MH):
                dve.scalar_tensor_tensor(mixT[:, h, T:TT], m_ps[:, h, :], cols[:, 16 + h:17 + h], zT[:, ZO + h, T:TT],
                                         ALU.mult, ALU.mult)
            dve.tensor_copy(mixT[:, 4:8, T:TT], m_ps[:, 4:8, :]).then_inc(mixs_ready, 1)

            dve.wait_ge(dstate_out, 48)
            dve.drain()
            for m in range(3):
                dve.wait_ge(bias_hi, m + 1)
                raw, hi = e_bias[m][32:64, :], e_bias_tmp_r[m].bitcast(F32)
                dve.tensor_tensor(e_bias_r[m][32:64, :], raw, hi, ALU.subtract).then_inc(bias_lo, 1)
            for i in range(NTILE):
                r = rows(i)
                dve.wait_ge(y_psum, i + 1)
                if i < EARLY:
                    dve.wait_ge(early_x, i + 1)
                else:
                    dve.wait_ge(xr_in[i % 2], 16 * (i // 2 + 1))
                for q in range(2):
                    cs = slice(512 * q, 512 * q + 512)
                    other = y1[0:r, i, cs] if i < EARLY else xbuf[0:r, i % 2, cs]
                    last = dve.tensor_tensor(y1[0:r, i, cs], other, ps[2 * (i % 2) + q][0:r, :], ALU.add)
                last.then_inc(y_ready, 1)
                if i == 0:
                    dve.wait_ge(iotas_made, 1)
                    dve.wait_ge(late_in, 64)
                dve.wait_ge(rms2_ready, i + 1)
                dve.reciprocal(ssq[0:r, i:i + 1], ssq[0:r, i:i + 1])
                dve.drain()
                if i >= 2:
                    dve.wait_ge(xhat_out[i % 2], 16 * (i // 2))
                dve.scalar_tensor_tensor(xhat[0:r, i % 2, :], y1[0:r, i, :], ssq[0:r, i:i + 1], n2_bc[0:r, :], ALU.mult,
                                         ALU.mult).then_inc(xhat_ready, 1)
                for q in range(2):
                    dve.wait_ge(x2_psum, 2 * i + q + 1)
                    dve.tensor_copy(x2T[:, 4 * q:4 * q + 4, 0:r],
                                    ps[4 + q][:, :].rearrange("p (c t) -> p c t", c=4)[:, :, 0:r]).then_inc(x2_ready, 1)
                dve.wait_ge(lg_psum, i + 1)
                dve.tensor_tensor(lg[0:r, :], ps[6][0:r, 0:NE], br_bc[0:r, :], ALU.add)
                dve.drain()
                dve.max(top8[0:r, :], lg[0:r, :])
                dve.drain()
                dve.max_index(idx8[0:r, :], top8[0:r, :], lg[0:r, :])
                dve.tensor_scalar(rs1[0:r, 0:1], top8[0:r, 0:1], -1.0, None, ALU.mult).then_inc(top_ready, 1)
                dve.drain()
                dve.tensor_copy(idxf[0:r, :], idx8[0:r, :])
                dve.drain()
                dve.tensor_tensor(rt_oh[0:r], iota_e[0:r].unsqueeze(2).to_broadcast([r, NE, TOPK]),
                                  idxf[0:r, 0:TOPK].unsqueeze(1).to_broadcast([r, NE, TOPK]), ALU.is_equal)
                dve.drain()
                dve.tensor_reduce(chosen[0:r, i, :], rt_oh[0:r], AX_X, ALU.add)
                dve.tensor_tensor(rt_tmp[0:r], rt_oh[0:r],
                                  tok_k[0:r, i, :].unsqueeze(1).to_broadcast([r, NE, TOPK]), ALU.mult)
                dve.drain()
                dve.tensor_reduce(route_v[0:r, i, 0:NE, 1], rt_tmp[0:r], AX_X, ALU.add)
                dve.wait_ge(gexp_ready, i + 1)
                dve.reciprocal(rs1[0:r, 2:3], rs1[0:r, 1:2])
                dve.drain()
                dve.tensor_scalar(gate4[0:r, :], gexp[0:r, :], rs1[0:r, 2:3], None, ALU.mult)
                dve.drain()
                dve.tensor_tensor(rt_tmp[0:r], rt_oh[0:r],
                                  gate4[0:r, :].unsqueeze(1).to_broadcast([r, NE, TOPK]), ALU.mult)
                dve.drain()
                dve.tensor_reduce(route_v[0:r, i, 0:NE, 2], rt_tmp[0:r], AX_X, ALU.add)
                dve.drain()
            dve.tensor_copy(route_v[:, :, NE, 1:3], route_v[:, :, 0, 1:3]).then_inc(sel_ready, 1)
            dve.wait_ge(rank_psum, 1)
            before, totals = (ps[6][:, c:c + NTILE * NE].rearrange("p (i e) -> p i e", i=NTILE) for c in (64, 224))
            dve.tensor_copy(sums, totals)
            dve.drain()
            for i in range(1, NTILE):
                dve.tensor_tensor(sums[:, i, :], sums[:, i, :], sums[:, i - 1, :], ALU.add)
                dve.drain()
            dve.tensor_reduce(count_f[0:1, :], sums[0:1, NTILE - 1, :], AX_X, ALU.max)
            dve.tensor_copy(rank[:, 0, 0:NE], before[:, 0, :])
            dve.tensor_tensor(rank[:, 1:NTILE, 0:NE], before[:, 1:NTILE, :], sums[:, 0:NTILE - 1, :], ALU.add)
            dve.drain()
            dve.scalar_tensor_tensor(rank[:, :, 0:NE], rank[:, :, 0:NE], 1.0, chosen, ALU.add, ALU.mult)
            dve.tensor_copy(count_i[0:1, 0:1], count_f[0:1, :])
            dve.drain()
            dve.tensor_scalar(rank[:, :, 0:NE], rank[:, :, 0:NE], -1.0, None, ALU.add)
            dve.drain()
            dve.tensor_scalar(rank[:, :, NE:NE + 1], rank[:, :, 0:1], -float(CAP), None, ALU.add)
            dve.drain()
            dve.engine_nop().then_inc(count_ready, 1)

            def one_hot(u, e):
                for i in range(NTILE):
                    r = rows(i)
                    last = dve.tensor_scalar(onehot[0:r, u, i, :], iota_cap[0:r, :], rank[0:r, i, e], None, ALU.is_equal)
                last.then_inc(onehot_ready, 1)

            def slots(u, t):
                dve.wait_ge(list_psum, t + 1)
                l_ps = ps[4][0:CAP, 0:3]
                dve.tensor_copy(slot_gate[0:CAP, u:u + 1], l_ps[:, 2:3])
                dve.tensor_scalar(slot_tmp[0:CAP, u:u + 1], l_ps[:, 1:2], 0.0, BIG, ALU.is_equal, ALU.mult)
                dve.drain()
                dve.tensor_tensor(slot_tok[0:CAP, u:u + 1], l_ps[:, 0:1], slot_tmp[0:CAP, u:u + 1], ALU.add)
                dve.scalar_tensor_tensor(slot_dst[0:CAP, u:u + 1], l_ps[:, 1:2], -1.0, slot_tmp[0:CAP, u:u + 1],
                                         ALU.add, ALU.add).then_inc(slots_ready, 1)

            def rest_of_blocks(out, bank, q0, q1):
                for q in range(q0, q1):
                    last = dve.tensor_tensor(out[:, 1, 4 * q:4 * q + 4, :],
                                             ps[bank + q][:, 0:4 * CAP].rearrange("p (c n) -> p c n", c=4),
                                             out[:, 0, 4 * q:4 * q + 4, :].bitcast(F32), ALU.subtract)
                return last

            def rest_of_piece(k, p12):
                dve.wait_ge(hi_ready, p12 + (k + 1))
                split(dve, k).then_inc(lo_ready, 1)

            def picks(u, e):
                dve.tensor_copy(pick[:, u, :], id64[:, e].to_broadcast([64, CAP])).then_inc(pick_ready, 1)

            one_hot(0, slice(0, 1))
            picks(0, slice(0, 1))
            slots(0, 0)
            for k in range(AHEAD):
                rest_of_piece(k, 0)
            dve.wait_ge(xhi_ready, 1)
            rest_of_blocks(eX, 6, 0, 2).then_inc(ex_ready, 1)
            most = dve.value_load(count_i[0:1, 0:1], min_val=0, max_val=TT)
            with dve.Fori(0, PASSES) as again:
                with dve.If(again * CAP < most):
                    with dve.Fori(0, NE // 2) as pair:
                        t0 = dve.snap(again * NE + pair * 2)
                        t8, p12 = dve.snap(t0 * 8), dve.snap(t0 * N_PIECE)
                        for u in range(2):
                            t, k = t0 + u, N_PIECE * u
                            one_hot(1 - u, bass.ds(pair * 2 + (u + 1), 1))
                            for n in range(3, 7):
                                rest_of_piece(k + n, p12)
                            dve.wait_ge(pieces_used, p12 + (N_FIRST + k + 4))
                            for q in range(2):
                                last = dve.tensor_scalar(eG[0:CAP, 512 * q:512 * q + 512], ps[q][0:CAP, :], LIMIT, None, ALU.min)
                            last.then_inc(g_ready, 1)
                            dve.wait_ge(yrow_ready, t + 1)
                            dve.wait_ge(rows_out[1 - u], t8 + 16)
                            slots(1 - u, t + 1)
                            picks(1 - u, bass.ds(pair * 2 + (u + 1), 1))
                            rest_of_piece(k + 7, p12)
                            dve.wait_ge(sg_ready, t + 1)
                            dve.tensor_tensor(eS[0:CAP, :], eS[0:CAP, :], eG[0:CAP, :], ALU.mult)
                            for q in range(2):
                                dve.wait_ge(pieces_used, p12 + (N_FIRST + k + 6 + 2 * q))
                                cs = slice(512 * q, 512 * q + 512)
                                dve.tensor_scalar(hrow[0:CAP, cs], ps[2 + q][0:CAP, :], LIMIT, -LIMIT, ALU.min, ALU.max)
                                dve.drain()
                                dve.scalar_tensor_tensor(hrow[0:CAP, cs], hrow[0:CAP, cs], 1.0, eS[0:CAP, cs], ALU.add,
                                                         ALU.mult).then_inc(h_ready, 1)
                                if q == 0:
                                    rest_of_piece(k + 8, p12)
                                rest_of_piece(k + 9 + q, p12)
                                if q == 0:
                                    dve.wait_ge(hhi_ready, t * 2 + 1)
                                    rest_of_blocks(eH, 0, 0, 1).then_inc(hlo_ready, 1)
                            dve.wait_ge(xhi_ready, t + 2)
                            rest_of_blocks(eX, 6, 0, 2).then_inc(ex_ready, 1)
                            dve.wait_ge(hhi_ready, t * 2 + 2)
                            rest_of_blocks(eH, 0, 1, 2).then_inc(hlo_ready, 1)
                            for n in range(11, 15):
                                rest_of_piece(k + n, p12)
                    dve.tensor_scalar(rank[:, :, :], rank[:, :, :], -float(CAP), None, ALU.add)
                    dve.drain()

            def final_sum(n):
                i = FINAL[n]
                r = rows(i)
                dve.wait_ge(last_in[i], 16)
                dve.tensor_tensor(y_all[0:r, i, 0:1024], y_all[0:r, i, 0:1024], y_all[0:r, i, 1024:2048], ALU.add)
                dve.drain()
                dve.tensor_tensor(y1[0:r, i, :], y1[0:r, i, :], y_all[0:r, i, 0:1024], ALU.add)
                dve.drain()
                dve.wait_ge(pair_ready, n + 1)
                dve.tensor_tensor(y1[0:r, i, :], y1[0:r, i, :], y_all[0:r, i, 2048:3072], ALU.add).then_inc(fsum_ready, 1)

            final_sum(0)
            for n, i in enumerate(FINAL):
                r = rows(i)
                if n + 1 < NTILE:
                    final_sum(n + 1)
                dve.wait_ge(frms_ready, n + 1)
                dve.reciprocal(ssq[0:r, i:i + 1], ssq[0:r, i:i + 1])
                dve.drain()
                dve.scalar_tensor_tensor(y1[0:r, i, :], y1[0:r, i, :], ssq[0:r, i:i + 1], fn_bc[0:r, :], ALU.mult,
                                         ALU.mult).then_inc(fin_ready, 1)

        @block.tensor
        def _(pe):
            def mm(out, lhsT, rhs, start=True, stop=True):
                return pe.matmul(out, lhsT, rhs, start=start, stop=stop, skip_group_check=True)

            def tr(out, in_, k):
                return pe.transpose(out, in_, ident[0:k, 0:k])

            def use(k):
                pe.wait_ge(*landed(k))

            pe.wait_ge(ident_made, 1)
            pe.wait_ge(consts_in, 16 * CONSTS)
            tr(ps[6][:, 0:20], reg_w[0:20, 0:P], 20).then_inc(gate_pe, 1)
            for i in range(NTILE):
                r = rows(i)
                pe.wait_ge(xn_ready, i + 1)
                for q in range(2):
                    if i:
                        pe.wait_ge(xT_ready, 2 * (i - 1) + q + 1)
                    for c in range(4):
                        last = tr(ps[4 + q][:, c * P:c * P + r],
                                  xbuf[0:r, i % 2, (4 * q + c) * P:(4 * q + c + 1) * P], r)
                    last.then_inc(xT_psum, 1)
            pe.wait_ge(xT_ready, 2 * NTILE)

            def ts_of(i):
                return slice(i * P, (i + 1) * P)

            tok_blocks = ([[(ZV + x, i) for x in range(MH)] for i in range(NT)]
                          + [[(ZK + x, 2 * q + i) for i in range(2) for x in range(2)] for q in range(2)]
                          + [[(ZAV, i) for i in range(NT)], [(ZAK, NT - 1)]])

            def token_major(n):
                if n >= 2:
                    pe.wait_ge(tok_ready, n - 1)
                if n == 1:
                    pe.wait_ge(*absf_ready)
                for x, (blk, i) in enumerate(tok_blocks[n]):
                    last = tr(ps[4 + 2 * (n % 2)][:, x * P:(x + 1) * P], zT[:, blk, ts_of(i)], P)
                last.then_inc(tok_psum, 1)

            for j in range(NZ + 1):
                pair = 2 * (j % 2)
                pe.wait_ge(w_lo, 1 + (j + 1) // 2)
                if j:
                    b = j - 1
                    parts = [v.rearrange("p (c n) -> p c n", c=KC)[:, :, (b % 2) * P:(b % 2 + 1) * P]
                             for v in (rounded_r(b // 2 - N_FIRST), rest_r(b // 2 - N_FIRST))]
                else:
                    parts = [wif_r[:, n] for n in range(2)]
                if j >= 2:
                    pe.wait_ge(proj_ready, j - 1)
                hi, lo = parts
                for c in range(KC):
                    for half in range(2):
                        out, cs = ps[pair + half][0:hi.shape[2], 0:HALF], slice(half * HALF, (half + 1) * HALF)
                        mm(out, hi[:, c, :], xnT_hi[:, c, cs], start=(c == 0), stop=False)
                        mm(out, hi[:, c, :], xnT_lo[c][:, cs], start=False, stop=False)
                        last = mm(out, lo[:, c, :], xnT_hi[:, c, cs], start=False, stop=(c == KC - 1))
                last.then_inc(proj_psum, 1)
                if j and b % 2:
                    pe.wait_ge(proj_psum, j + 1)
                    tr(ps[7][0:1, 0:1], ident[0:1, 0:1], 1).then_inc(pieces_used, 1)
                if j == 2:
                    pe.wait_ge(proj_ready, 1)
                    mm(ps[6][0:4, :], ident[0:8, 4:8], gates[:, 0:T]).then_inc(gate_pe, 1)
                if j == 8:
                    pe.wait_ge(*grows_ready)
                    for i in range(NT):
                        ts = slice(i * P, (i + 1) * P)
                        tr(ps[5][:, i * 4:i * 4 + 4], g_rows[1][0:4, ts], 4)
                        last = tr(ps[5][:, 16 + i * 4:20 + i * 4], g_rows[3][0:4, ts], 4)
                    last.then_inc(gate_pe, 1)
                if TOK_AT <= j < TOK_AT + 6:
                    token_major(j - TOK_AT)

            pe.wait_ge(proj_ready, NZ + 1)
            order = [ZQ, ZQ + 1, ZK, ZK + 1, ZV, ZV + 1, ZV + 2, ZV + 3, ZAQ, ZAQ + 1, ZAQ + 2, ZAQ + 3, ZAK, ZAV]
            for n in range(4):
                if n >= 2:
                    pe.wait_ge(zs_ready, n - 1)
                blocks = order[4 * n:4 * n + 4]
                for x, b in enumerate(blocks):
                    last = tr(ps[n % 2][0:NB, x * P:(x + 1) * P], zT[:, b, T:TT], P)
                if n == 3:
                    last = tr(ps[1][0:NB, 256:264], gates[:, T:TT], 8)
                last.then_inc(zs_psum, 1)
            token_major(6)
            token_major(7)
            pe.wait_ge(*gtok_ready)

            pe.wait_ge(tok_ready, 8)
            pe.wait_ge(zs_ready, 4)

            def scores(h, kb):
                n = NT * h + kb + 1
                rs, blk = slice((h % 2) * DK, (h % 2) * DK + DK), h // 2
                if n > 2:
                    pe.wait_ge(wgt_ready, n - 2)
                mm(ps[4 + (n - 1) % 2][:, 0:T - kb * P], zT[rs, ZK + blk, kb * P:(kb + 1) * P],
                   zT[rs, ZQ + blk, kb * P:T]).then_inc(score_psum, 1)

            def minus_m(h):
                pe.wait_ge(gs_ready, h)
                mm(ps[0][:, :], negsel[:, h * P:(h + 1) * P], gates[0:4, 0:T]).then_inc(negm_psum, 1)

            minus_m(0)
            scores(0, 0)
            for h in range(MH):
                for kb in range(NT):
                    n = NT * h + kb + 1
                    if kb + 1 < NT:
                        scores(h, kb + 1)
                    if kb == 2 and h + 1 < MH:
                        minus_m(h + 1)
                    pe.wait_ge(wgt_ready, n)
                    if kb == 0:
                        pe.wait_ge(num_used, h)
                    for i in range(kb, NT):
                        last = mm(ps[6 + i // 2][:, (i % 2) * (DV + 1):(i % 2 + 1) * (DV + 1)],
                                  wexp[:, (n - 1) % 2, (i - kb) * P:(i - kb + 1) * P], v_tok[:, kb, h, :],
                                  start=(kb == 0 and i % 2 == 0), stop=(kb == i))
                    last.then_inc(num_kb, 1)
                tr(ps[3][0:1, 0:1], ident[0:1, 0:1], 1).then_inc(num_psum, 1)
                if h + 1 < MH:
                    scores(h + 1, 0)
                pe.wait_ge(kg_ready, h + 1)
                pe.wait_ge(state_ready, h)
                for kb in range(NT):
                    last = mm(ps[1][0:DK, 0:DV + 1], kg[:, kb, :], v_tok[:, kb, h, :], start=(kb == 0), stop=(kb == NT - 1))
                last.then_inc(state_psum, 1)
            for h in range(MH):
                pe.wait_ge(hn_ready, h + 1)
                if h >= 2:
                    pe.wait_ge(mixm_ready, h - 1)
                for i in range(NT):
                    last = tr(ps[2 + h % 2][:, i * P:(i + 1) * P], h_rows[h][:, i * P:(i + 1) * P], P)
                last.then_inc(hT_psum, 1)

            def early(i):
                for c in range(MH):
                    k = N_IN + c // 2
                    use(k)
                    w = piece(k).rearrange("p (c n) -> p c n", c=2)
                    for q in range(2):
                        last = mm(ps[q][:, :], mixT[:, c, ts_of(i)], w[:, c % 2, q * 512:(q + 1) * 512],
                                  start=(c == 0), stop=(c == MH - 1))
                last.then_inc(early_psum, 1)

            pe.wait_ge(mixm_ready, MH)
            early(0)
            pe.wait_ge(*dw_ready)
            pe.wait_ge(dec_in, 16 * DEC_IN)
            mm(ps[4][:, 0:130], r4, r32[:, 0:130]).then_inc(sample_pe, 1)
            pe.wait_ge(*dpart_ready)
            mm(ps[5][0:32, 0:130], g4, part2).then_inc(sample_pe, 1)
            pe.wait_ge(*q2_ready)
            mm(ps[3][0:64, 0:130], r8, brow9[:, 0:130])
            mm(ps[3][0:64, 256:384], r4[0:16, 0:64], kv16)
            tr(ps[3][:, 384:448], q2, 64).then_inc(sample_pe, 1)
            pe.wait_ge(early_ready, 1)
            early(1)
            pe.wait_ge(*qbd_ready)
            pe.wait_ge(cache_in, 32)
            pe.wait_ge(*vrep_ready)
            pe.wait_ge(hn_ready, MH)

            def sample_scores(b):
                pe.wait_ge(kc_ready, b + 1)
                mm(ps[7][:, b * 8:b * 8 + 8], kT_s[:, b % 2, :], qbd[:, b * 8:b * 8 + 8]).then_inc(ks_psum, 1)

            for b in range(NB):
                if b >= 2:
                    pe.wait_ge(kc_ready, b - 1)
                tr(ps[4 + 2 * (b % 2)][:, 0:P], cache_ks[:, b, :], P).then_inc(kc_psum, 1)
                if b:
                    sample_scores(b - 1)
            sample_scores(NB - 1)
            pe.wait_ge(*sT_ready)
            pe.wait_ge(*dh_ready)
            tr(ps[5][0:64, 0:P], sT, P).then_inc(sample_pe, 1)
            pe.wait_ge(*dprob_ready)
            tr(ps[5][:, 256:320], dl[:, 0:P], 64).then_inc(sample_pe, 1)
            pe.wait_ge(*dpT_ready)
            for b in range(NB):
                last = mm(ps[6][:, 256 + b * 8:264 + b * 8], cache_vs[:, b, :], pT[:, b * 8:b * 8 + 8])
            last.then_inc(sample_pe, 1)
            pe.wait_ge(*doT_ready)
            tr(ps[7][0:64, P:2 * P], oT, P).then_inc(sample_pe, 1)

            pe.wait_ge(aksw_in, 32)
            pe.wait_ge(*datt_ready)
            pe.wait_ge(mixm_ready, MH)

            def att_scores(n):
                i, h = divmod(n - 1, AH)
                rs, g = slice((h % 2) * HD, (h % 2) * HD + HD), h // GRP
                keys = zT[rs, ZAK, 0:T] if g == h % 2 else ak_swap[rs, :]
                c, lo = (n - 1) % 2, (P if i == 0 else 0)
                if n > 2:
                    pe.wait_ge(logit_ready, n - 2)
                mm(ps[4 + c][:, lo:256], zT[rs, ZAQ + h // 2, i * P:(i + 1) * P],
                   keys[:, (i - 1) * P + lo:(i + 1) * P]).then_inc(s_psum, 1)

            def att_pT(n):
                i = (n - 1) // AH
                c = (n - 1) % 2
                pe.wait_ge(prob_ready, n)
                if n > 2:
                    pe.wait_ge(pT_ready, n - 2)
                for kb in range(1 if i == 0 else 0, 2):
                    last = tr(ps[2 + c][:, kb * P:(kb + 1) * P], prob[:, c, kb * P:(kb + 1) * P], P)
                last.then_inc(pT_psum, 1)

            def att_pv(n):
                i, h = divmod(n - 1, AH)
                g, c = h // GRP, (n - 1) % 2
                pe.wait_ge(pT_ready, n)
                if h == 0 and i >= 2:
                    pe.wait_ge(otok_ready, i - 1)
                first = 1 if i == 0 else 0
                for kb in range(first, 2):
                    last = mm(ps[6 + i % 2][:, h * HD:(h + 1) * HD], probT[:, c, kb * P:(kb + 1) * P],
                              av_tok[:, i - 1 + kb, g * HD:(g + 1) * HD], start=(kb == first), stop=(kb == 1))
                last.then_inc(pv_psum, 1)
                if h == AH - 1:
                    pe.wait_ge(otok_ready, i + 1)
                    if i >= 2:
                        pe.wait_ge(mixa_ready, i - 1)
                    for c4 in range(4):
                        last = tr(ps[i % 2][:, c4 * P:(c4 + 1) * P], o_tok[:, c4 * P:(c4 + 1) * P], P)
                    last.then_inc(oT_psum, 1)

            units = NT * AH
            att_scores(1)
            att_scores(2)
            for n in range(1, units + 1):
                if n + 2 <= units:
                    att_scores(n + 2)
                att_pT(n)
                if n % AH != 1:
                    att_pv(n - 1)
                if n % AH == 0:
                    att_pv(n)
            pe.wait_ge(mixs_in, 16)
            pe.wait_ge(pT_ready, units)
            for c in range(KC):
                last = tr(ps[3][:, c * NB:(c + 1) * NB], mix_s[:, c * P:(c + 1) * P], NB)
            last.then_inc(mixs_psum, 1)

            pe.wait_ge(mixa_ready, NT)
            pe.wait_ge(mixs_ready, 1)

            def project(i):
                r = rows(i)
                if i >= 2:
                    pe.wait_ge(y_ready, i - 1)
                first = MH if i < EARLY else 0
                for c in range(first, KC):
                    if c == (first + KC) // 2 and i:
                        route(i - 1)
                    k = N_IN + c // 2
                    use(k)
                    w = piece(k).rearrange("p (c n) -> p c n", c=2)
                    for q in range(2):
                        last = mm(ps[2 * (i % 2) + q][0:r, :], mixT[:, c, i * P:i * P + r],
                                  w[:, c % 2, q * 512:(q + 1) * 512], start=(c == first), stop=(c == KC - 1))
                last.then_inc(y_psum, 1)

            def route(i):
                r = rows(i)
                pe.wait_ge(xhat_ready, i + 1)
                for q in range(2):
                    if i:
                        pe.wait_ge(x2_ready, 2 * (i - 1) + q + 1)
                    for c in range(4):
                        last = tr(ps[4 + q][:, c * P:c * P + r], xhat[0:r, i % 2, (4 * q + c) * P:(4 * q + c + 1) * P], r)
                    last.then_inc(x2_psum, 1)
                pe.wait_ge(x2_ready, 2 * i + 2)
                pe.wait_ge(late_in, 64)
                pe.wait_ge(top_ready, i)
                for c in range(KC):
                    last = mm(ps[6][0:r, 0:NE], x2T[:, c, 0:r], w_rt[:, c, :], start=(c == 0), stop=(c == KC - 1))
                last.then_inc(lg_psum, 1)

            for i in range(NTILE):
                project(i)
            for k in range(N_OUT):
                tr(ps[7][0:1, 0:1], ident[0:1, 0:1], 1).then_inc(pieces_used, 1)
            route(NTILE - 1)

            pe.wait_ge(sel_ready, 1)
            every = chosen.rearrange("p i e -> p (i e)")
            mm(ps[6][:, 64:64 + NTILE * NE], tri, every)
            mm(ps[6][:, 224:224 + NTILE * NE], ones, every).then_inc(rank_psum, 1)

            def make_list(u, t, e):
                pe.wait_ge(onehot_ready, t + 1)
                if u or not isinstance(t, int):
                    pe.wait_ge(yrow_ready, t)
                for i in range(NTILE):
                    r = rows(i)
                    last = mm(ps[4][0:CAP, 0:3], onehot[0:r, u, i, :],
                              route_v[0:r, i, e, :].rearrange("p a c -> p (a c)"), start=(i == 0), stop=(i == NTILE - 1))
                last.then_inc(list_psum, 1)

            def transpose_rows(u, landed_rows):
                pe.wait_ge(rows_in[u], landed_rows)
                for c in range(KC):
                    last = tr(ps[6 + c // 4][:, (c % 4) * CAP:(c % 4 + 1) * CAP], xg[0:CAP, u, c * P:(c + 1) * P], CAP)
                last.then_inc(ex_psum, 1)

            def transpose_h(q, t):
                pe.wait_ge(h_ready, t * 2 + (q + 1))
                for c in range(4):
                    last = tr(ps[q][:, c * CAP:(c + 1) * CAP], hrow[0:CAP, (4 * q + c) * P:(4 * q + c + 1) * P], CAP)
                last.then_inc(hT_psum2, 1)

            def bias_rows_of(m, bank, u):
                for q in range(2):
                    mm(ps[bank + q][0:CAP, :], pick[:, u, :], e_bias_r[m][:, 512 * q:512 * q + 512], stop=False)

            def product(k, bank, x, p12):
                pe.wait_ge(lo_ready, p12 + (k + 1))
                halves = k % N_PIECE // 4 == 1
                n = 4 if halves else 2
                hi = rounded_r(k).rearrange("p (c n) -> p c n", c=n)
                lo = rest_r(k).rearrange("p (c n) -> p c n", c=n)
                for cc in range(n):
                    c = 4 * (k % 2) + cc if halves else 2 * (k % 4) + cc
                    for q in [k % 4 // 2] if halves else [0, 1]:
                        cs = slice(0, 512) if halves else slice(512 * q, 512 * q + 512)
                        out = ps[bank + q][0:CAP, :]
                        mm(out, x[:, 0, c, :], hi[:, cc, cs], start=False, stop=False)
                        mm(out, x[:, 1, c, :], hi[:, cc, cs], start=False, stop=False)
                        last = mm(out, x[:, 0, c, :], lo[:, cc, cs], start=False, stop=(c == KC - 1))
                last.then_inc(pieces_used, 1)

            pe.wait_ge(count_ready, 1)
            make_list(0, 0, slice(0, 1))
            transpose_rows(0, 16)
            most = pe.value_load(count_i[0:1, 0:1], min_val=0, max_val=TT)
            with pe.Fori(0, PASSES) as again:
                with pe.If(again * CAP < most):
                    with pe.Fori(0, NE // 2) as pair:
                        t0 = pe.snap(again * NE + pair * 2)
                        t8, p12 = pe.snap(t0 * 8), pe.snap(t0 * N_PIECE)
                        for u in range(2):
                            t, k = t0 + u, N_PIECE * u
                            pe.wait_ge(ex_ready, t + 1)
                            pe.wait_ge(pick_ready, t + 1)
                            bias_rows_of(0, 0, u)
                            for n in range(4):
                                product(k + n, 0, eX, p12)
                            make_list(1 - u, t + 1, bass.ds(pair * 2 + (u + 1), 1))
                            bias_rows_of(1, 2, u)
                            for n in range(4, 7):
                                product(k + n, 2, eX, p12)
                            pe.wait_ge(g_ready, t + 1)
                            transpose_h(0, t)
                            product(k + 7, 2, eX, p12)
                            transpose_rows(1 - u, t8 + (16 if u == 0 else 32))
                            pe.wait_ge(slots_ready, t + 2)
                            pe.wait_ge(hlo_ready, t * 2 + 1)
                            bias_rows_of(2, 4, u)
                            product(k + 8, 4, eH, p12)
                            transpose_h(1, t)
                            product(k + 9, 4, eH, p12)
                            pe.wait_ge(hlo_ready, t * 2 + 2)
                            product(k + 10, 4, eH, p12)
                            product(k + 11, 4, eH, p12)


_INS = ["x_prompt", "x_sample", "state_C", "state_n", "state_m", "cache_k", "cache_v", "rel_bias", "norm1", "w_in",
        "b_if", "m_gain", "sinks", "w_out", "norm2", "w_router", "b_router", "w_gate", "b_gate", "w_up", "b_up",
        "w_down", "b_down", "final_norm"]
_OUTS = {"y_prompt": (1, T, D), "y_sample": (NB, 1, D), "p_C": (1, 1, MH, DK, DV), "p_n": (1, 1, MH, DK),
         "p_m": (1, 1, MH), "p_k": (1, 1, WIN, KV, HD), "p_v": (1, 1, WIN, KV, HD), "s_C": (1, NB, MH, DK, DV),
         "s_n": (1, NB, MH, DK), "s_m": (1, NB, MH), "s_k": (1, NB, WIN, KV, HD), "s_v": (1, NB, WIN, KV, HD)}


def kernel(**inputs):
    import numpy as np
    import concourse.bacc as bacc
    from concourse.bass_utils import run_bass_kernel_spmd as run

    nc = bacc.Bacc("TRN2", target_bir_lowering=False, num_devices=1)
    arrays, ins, outs = {}, {}, {}
    for name in _INS:
        x = np.ascontiguousarray(inputs[name])
        arrays[f"in_{name}"] = x
        ins[name] = nc.dram_tensor(f"in_{name}", x.shape, mybir.dt.from_np(x.dtype), kind="ExternalInput").ap()
    for name, shape in _OUTS.items():
        outs[name] = nc.dram_tensor(f"out_{name}", shape, F32, kind="ExternalOutput").ap()
    hybrid_step(nc, ins, outs)
    r = run(nc, [arrays], core_ids=[0])
    return tuple(r.results[0][f"out_{name}"] for name in _OUTS)
```
